# Optimizing a Trainium2 kernel written in Bass

```python
import jax, jax.numpy as jnp
from jax import lax
import numpy as np

D_MODEL = 1024
BATCH = 1
SEQ = 256
DEPTH = 1

HEAD_DIM = 64
MIX_WIDTH = D_MODEL
RWKV_WIDTH = MIX_WIDTH // 2
MOBA_WIDTH = MIX_WIDTH - RWKV_WIDTH
RWKV_HEADS = RWKV_WIDTH // HEAD_DIM
MOBA_HEADS = MOBA_WIDTH // HEAD_DIM
DECAY_LORA = max(32, int(round(1.8 * D_MODEL ** 0.5 / 32)) * 32)
AAA_LORA = max(32, int(round(1.8 * D_MODEL ** 0.5 / 32)) * 32)
GATE_LORA = max(32, int(round(0.6 * D_MODEL ** 0.8 / 32)) * 32)
RWKV_LN_EPS = 64e-5
RWKV_PROJ = 3 * RWKV_WIDTH + DECAY_LORA + AAA_LORA + GATE_LORA
MOBA_PROJ = 3 * MOBA_WIDTH
IN_COLS = RWKV_PROJ + MOBA_PROJ
MOBA_BLOCK = 256
MOBA_TOPK = 3
MOBA_QUERY_CHUNK = 16
N_EXPERTS = 32
TOP_K = 4
D_FF = D_MODEL
SWIGLU_LIMIT = 7.0
SWIGLU_ALPHA = 1.702
EXPERT_ROWS = 128
NORM_EPS = 1e-6


def rms_norm(x, g):
    xf = x.astype(jnp.float32)
    y = xf * lax.rsqrt(jnp.mean(xf * xf, axis=-1, keepdims=True) + NORM_EPS)
    return (y * g.astype(jnp.float32)).astype(x.dtype)

def token_shift(p):
    return jnp.pad(p, ((0, 0), (1, 0), (0, 0)))[:, :-1]

def rwkv7_time_mix(p, mu, w0, w_up, a0, a_up, g_up, k_k, k_a, r_k, ln_g, ln_b):
    B, S, _ = p.shape
    H, N, W = RWKV_HEADS, HEAD_DIM, RWKV_WIDTH
    f32 = jnp.float32
    p = p + (token_shift(p) - p) * mu
    r, k, v, xw, xa, xg = jnp.split(
        p, [W, 2 * W, 3 * W, 3 * W + DECAY_LORA, 3 * W + DECAY_LORA + AAA_LORA], axis=-1)
    w_log = -jax.nn.softplus(-(w0 + jnp.tanh(xw) @ w_up)) - 0.5
    decay = jnp.exp(-jnp.exp(w_log.astype(f32)))
    a = jax.nn.sigmoid(a0 + xa @ a_up)
    g = jax.nn.sigmoid(xg) @ g_up
    heads = lambda t: t.reshape(B, S, H, N).astype(f32)
    kk = heads(k * k_k)
    kk = kk / jnp.maximum(jnp.linalg.norm(kk, axis=-1, keepdims=True), 1e-12)
    k = k * (1.0 + (a - 1.0) * k_a)
    r_h, k_h, v_h, w_h, a_h = heads(r), heads(k), heads(v), heads(decay), heads(a)

    def step(state, inp):
        r_t, w_t, k_t, v_t, kk_t, a_t = inp
        sa = jnp.einsum('bhij,bhj->bhi', state, -kk_t)
        state = (state * w_t[:, :, None, :]
                 + sa[..., None] * (kk_t * a_t)[:, :, None, :]
                 + v_t[..., None] * k_t[:, :, None, :])
        y_t = jnp.einsum('bhij,bhj->bhi', state, r_t)
        return state, y_t

    sf = lambda t: jnp.moveaxis(t, 1, 0)
    state0 = jnp.zeros((B, H, N, N), f32)
    _, y = lax.scan(step, state0, (sf(r_h), sf(w_h), sf(k_h), sf(v_h), sf(kk), sf(a_h)))
    y = jnp.moveaxis(y, 0, 1)
    mean = jnp.mean(y, axis=-1, keepdims=True)
    var = jnp.mean(jnp.square(y - mean), axis=-1, keepdims=True)
    y = ((y - mean) * lax.rsqrt(var + RWKV_LN_EPS)).reshape(B, S, W) * ln_g + ln_b
    bonus = jnp.sum(r_h * k_h * r_k, axis=-1, keepdims=True) * v_h
    y = (y + bonus.reshape(B, S, W)) * g
    return y.astype(p.dtype)

def moba_attention(p, q_norm_g, k_norm_g):
    B, S, _ = p.shape
    H, N, BLK, QC = MOBA_HEADS, HEAD_DIM, MOBA_BLOCK, MOBA_QUERY_CHUNK
    f32 = jnp.float32
    to_heads = lambda t: t.reshape(B, S, H, N).transpose(0, 2, 1, 3)
    q, k, v = [to_heads(t) for t in jnp.split(p, 3, axis=-1)]
    q = rms_norm(q, q_norm_g)
    k = rms_norm(k, k_norm_g)
    NB = -(-S // BLK)
    n_sel = min(MOBA_TOPK, NB)
    pad = NB * BLK - S
    kb = jnp.pad(k, ((0, 0), (0, 0), (0, pad), (0, 0))).reshape(B, H, NB, BLK, N)
    vb = jnp.pad(v, ((0, 0), (0, 0), (0, pad), (0, 0))).reshape(B, H, NB, BLK, N)
    kmean = jnp.mean(kb.astype(f32), axis=3)
    slopes = jnp.exp2(-8.0 * (jnp.arange(H, dtype=f32) + 1.0) / H)
    scale = HEAD_DIM ** -0.5
    bi = jnp.arange(B)[:, None, None, None]
    hi = jnp.arange(H)[None, :, None, None]
    n_chunks = S // QC
    q_chunks = jnp.moveaxis(q.reshape(B, H, n_chunks, QC, N), 2, 0)

    def attend_chunk(args):
        qi, ci = args
        t0 = ci * QC
        j = t0 // BLK
        tq = t0 + jnp.arange(QC)
        gate = jnp.einsum('bhqd,bhnd->bhqn', qi.astype(f32), kmean)
        gate = jnp.where(jnp.arange(NB) < j, gate, -jnp.inf)
        _, sel = lax.top_k(gate, n_sel)
        ksel = kb[bi, hi, sel]
        vsel = vb[bi, hi, sel]
        kpos_sel = sel[..., None] * BLK + jnp.arange(BLK)
        s_sel = (jnp.einsum('bhqd,bhqmkd->bhqmk', qi, ksel).astype(f32) * scale
                 - slopes[:, None, None, None] * (tq[:, None, None] - kpos_sel))
        s_sel = jnp.where((jnp.arange(n_sel) < j)[:, None], s_sel, -jnp.inf)
        k_own = lax.dynamic_index_in_dim(kb, j, axis=2, keepdims=False)
        v_own = lax.dynamic_index_in_dim(vb, j, axis=2, keepdims=False)
        kpos_own = j * BLK + jnp.arange(BLK)
        s_own = (jnp.einsum('bhqd,bhkd->bhqk', qi, k_own).astype(f32) * scale
                 - slopes[:, None, None] * (tq[:, None] - kpos_own[None, :]))
        s_own = jnp.where(kpos_own[None, :] <= tq[:, None], s_own, -jnp.inf)
        s = jnp.concatenate([s_sel.reshape(B, H, QC, n_sel * BLK), s_own], axis=-1)
        prob = jax.nn.softmax(s, axis=-1)
        p_sel = prob[..., :n_sel * BLK].reshape(B, H, QC, n_sel, BLK)
        p_own = prob[..., n_sel * BLK:]
        out = (jnp.einsum('bhqmk,bhqmkd->bhqd', p_sel, vsel)
               + jnp.einsum('bhqk,bhkd->bhqd', p_own, v_own))
        return out.astype(qi.dtype)

    out = lax.map(attend_chunk, (q_chunks, jnp.arange(n_chunks, dtype=jnp.int32)))
    out = jnp.moveaxis(out, 0, 2).reshape(B, H, S, N)
    return out.transpose(0, 2, 1, 3).reshape(B, S, MOBA_WIDTH)

def moe_ffn(h, w_router, b_router, w_gate_up, b_gate_up, w_down, b_down):
    T, D = h.shape
    logits = (h @ w_router + b_router).astype(jnp.float32)
    top_val, top_idx = lax.top_k(logits, TOP_K)
    weights = jax.nn.softmax(top_val, axis=-1)
    M = T * TOP_K
    slot_expert = top_idx.reshape(M)
    slot_token = jnp.arange(M, dtype=jnp.int32) // TOP_K
    slot_weight = weights.reshape(M)
    order = jnp.argsort(slot_expert)
    e_sorted = slot_expert[order]
    counts = jnp.bincount(slot_expert, length=N_EXPERTS)
    padded = (counts + EXPERT_ROWS - 1) // EXPERT_ROWS * EXPERT_ROWS
    pad_end = jnp.cumsum(padded)
    pad_start = pad_end - padded
    start = jnp.cumsum(counts) - counts
    dest = pad_start[e_sorted] + jnp.arange(M) - start[e_sorted]
    P = M + N_EXPERTS * EXPERT_ROWS
    n_blocks = P // EXPERT_ROWS
    buf_token = jnp.zeros((P,), jnp.int32).at[dest].set(slot_token[order])
    buf_weight = jnp.zeros((P,), jnp.float32).at[dest].set(slot_weight[order])
    blk_expert = jnp.minimum(
        jnp.searchsorted(pad_end, jnp.arange(n_blocks) * EXPERT_ROWS, side='right'), N_EXPERTS - 1)

    def expert_block(args):
        tok, e = args
        xb = h[tok]
        gu = xb @ w_gate_up[e] + b_gate_up[e]
        gate = jnp.minimum(gu[:, :D_FF], SWIGLU_LIMIT)
        up = jnp.clip(gu[:, D_FF:], -SWIGLU_LIMIT, SWIGLU_LIMIT)
        act = (up + 1.0) * gate * jax.nn.sigmoid(SWIGLU_ALPHA * gate)
        return act @ w_down[e] + b_down[e]

    y = lax.map(expert_block, (buf_token.reshape(n_blocks, EXPERT_ROWS), blk_expert)).reshape(P, D)
    return jax.ops.segment_sum(y * buf_weight[:, None], buf_token, num_segments=T)

def hybrid_layer(x, c, w_ada, b_ada, norm1_g, w_in, rwkv_mu, rwkv_w0, rwkv_w_up, rwkv_a0,
                 rwkv_a_up, rwkv_g_up, rwkv_k_k, rwkv_k_a, rwkv_r_k, rwkv_ln_g, rwkv_ln_b,
                 q_norm_g, k_norm_g, w_out, norm2_g, w_router, b_router, w_gate_up,
                 b_gate_up, w_down, b_down):
    B, S, D = x.shape
    mods = jax.nn.silu(c) @ w_ada + b_ada
    shift1, scale1, gate1, shift2, scale2, gate2 = jnp.split(mods[:, None, :], 6, axis=-1)
    h = rms_norm(x, norm1_g) * (1.0 + scale1) + shift1
    proj = h @ w_in
    y_rwkv = rwkv7_time_mix(proj[..., :RWKV_PROJ], rwkv_mu, rwkv_w0, rwkv_w_up, rwkv_a0,
                            rwkv_a_up, rwkv_g_up, rwkv_k_k, rwkv_k_a, rwkv_r_k,
                            rwkv_ln_g, rwkv_ln_b)
    y_moba = moba_attention(proj[..., RWKV_PROJ:], q_norm_g, k_norm_g)
    x = x + gate1 * (jnp.concatenate([y_rwkv, y_moba], axis=-1) @ w_out)
    h = rms_norm(x, norm2_g) * (1.0 + scale2) + shift2
    y = moe_ffn(h.reshape(B * S, D), w_router, b_router, w_gate_up, b_gate_up, w_down, b_down)
    return x + gate2 * y.reshape(B, S, D).astype(x.dtype)

def first_inputs(seed: int = 0) -> dict:
    key = jax.random.key(seed)
    ks = jax.random.split(key, 27)
    nrm = lambda k, shape, s: jax.random.normal(k, shape, jnp.float32) * s
    L = DEPTH
    return {
        'x': nrm(ks[0], (BATCH, SEQ, D_MODEL), 1.0),
        'c': nrm(ks[1], (BATCH, D_MODEL), 1.0),
        'w_ada': nrm(ks[2], (L, D_MODEL, 6 * D_MODEL), 0.5 * D_MODEL ** -0.5),
        'b_ada': nrm(ks[3], (L, 6 * D_MODEL), 0.02),
        'norm1_g': 1.0 + nrm(ks[4], (L, D_MODEL), 0.05),
        'w_in': nrm(ks[5], (L, D_MODEL, IN_COLS), D_MODEL ** -0.5),
        'rwkv_mu': jax.random.uniform(ks[6], (L, RWKV_PROJ), jnp.float32),
        'rwkv_w0': jax.random.uniform(ks[7], (L, RWKV_WIDTH), jnp.float32, minval=-6.0, maxval=0.0),
        'rwkv_w_up': nrm(ks[8], (L, DECAY_LORA, RWKV_WIDTH), 0.3 * DECAY_LORA ** -0.5),
        'rwkv_a0': nrm(ks[9], (L, RWKV_WIDTH), 0.5),
        'rwkv_a_up': nrm(ks[10], (L, AAA_LORA, RWKV_WIDTH), 0.5 * AAA_LORA ** -0.5),
        'rwkv_g_up': nrm(ks[11], (L, GATE_LORA, RWKV_WIDTH), GATE_LORA ** -0.5),
        'rwkv_k_k': 0.85 + nrm(ks[12], (L, RWKV_WIDTH), 0.05),
        'rwkv_k_a': 1.0 + nrm(ks[13], (L, RWKV_WIDTH), 0.05),
        'rwkv_r_k': nrm(ks[14], (L, RWKV_HEADS, HEAD_DIM), 0.1),
        'rwkv_ln_g': 1.0 + nrm(ks[15], (L, RWKV_WIDTH), 0.05),
        'rwkv_ln_b': nrm(ks[16], (L, RWKV_WIDTH), 0.02),
        'q_norm_g': 1.0 + nrm(ks[17], (L, HEAD_DIM), 0.05),
        'k_norm_g': 1.0 + nrm(ks[18], (L, HEAD_DIM), 0.05),
        'w_out': nrm(ks[19], (L, MIX_WIDTH, D_MODEL), MIX_WIDTH ** -0.5),
        'norm2_g': 1.0 + nrm(ks[20], (L, D_MODEL), 0.05),
        'w_router': nrm(ks[21], (L, D_MODEL, N_EXPERTS), D_MODEL ** -0.5),
        'b_router': nrm(ks[22], (L, N_EXPERTS), 0.01),
        'w_gate_up': nrm(ks[23], (L, N_EXPERTS, D_MODEL, 2 * D_FF), D_MODEL ** -0.5),
        'b_gate_up': nrm(ks[24], (L, N_EXPERTS, 2 * D_FF), 0.01),
        'w_down': nrm(ks[25], (L, N_EXPERTS, D_FF, D_MODEL), D_FF ** -0.5),
        'b_down': nrm(ks[26], (L, N_EXPERTS, D_MODEL), 0.01),
    }

def first_block(x, c, w_ada, b_ada, norm1_g, w_in, rwkv_mu, rwkv_w0, rwkv_w_up, rwkv_a0,
              rwkv_a_up, rwkv_g_up, rwkv_k_k, rwkv_k_a, rwkv_r_k, rwkv_ln_g, rwkv_ln_b,
              q_norm_g, k_norm_g, w_out, norm2_g, w_router, b_router, w_gate_up,
              b_gate_up, w_down, b_down):
    for l in range(DEPTH):
        x = hybrid_layer(x, c, w_ada[l], b_ada[l], norm1_g[l], w_in[l], rwkv_mu[l], rwkv_w0[l],
                         rwkv_w_up[l], rwkv_a0[l], rwkv_a_up[l], rwkv_g_up[l], rwkv_k_k[l],
                         rwkv_k_a[l], rwkv_r_k[l], rwkv_ln_g[l], rwkv_ln_b[l], q_norm_g[l],
                         k_norm_g[l], w_out[l], norm2_g[l], w_router[l], b_router[l],
                         w_gate_up[l], b_gate_up[l], w_down[l], b_down[l])
    return x


N_MIXERS = 2
N_MEM = 256
MEM_HEADS = 4
MEM_HD = 64
SB_HEADS = 12
SB_HD = 64
SB_BLOCK = 128
HG_HEADS = 6
HG_DK = 128
HG_DV = 128
HG_CHUNK = 64
D_FF_2 = 4 * D_MODEL
D_MIX = SB_HEADS * SB_HD + MEM_HEADS * MEM_HD
SB_PROJ = 3 * SB_HEADS * SB_HD + MEM_HEADS * MEM_HD
HG_PROJ = 2 * HG_HEADS * HG_DK + 2 * HG_HEADS * HG_DV + MEM_HEADS * MEM_HD
N_LAYERS_A = (DEPTH + N_MIXERS - 1) // N_MIXERS
N_LAYERS_B = (DEPTH + N_MIXERS - 2) // N_MIXERS
DN_ALPHA = (2 * DEPTH) ** 0.25
DN_BETA = (8 * DEPTH) ** -0.25
LN_EPS = 1e-5
RMS_EPS = 1e-6


def layer_norm(x, g, b):
    xf = x.astype(jnp.float32)
    mu = jnp.mean(xf, axis=-1, keepdims=True)
    var = jnp.mean(jnp.square(xf - mu), axis=-1, keepdims=True)
    return ((xf - mu) * lax.rsqrt(var + LN_EPS) * g + b).astype(x.dtype)

def split_heads(t, h):
    b, s, _ = t.shape
    return t.reshape(b, s, h, -1).transpose(0, 2, 1, 3)

def merge_heads(t):
    b, h, s, d = t.shape
    return t.transpose(0, 2, 1, 3).reshape(b, s, h * d)

def memory_attention(q_mem, mem, w_mem_kv):
    k, v = jnp.split(mem @ w_mem_kv, 2, axis=-1)
    q = split_heads(q_mem, MEM_HEADS)
    k = split_heads(k, MEM_HEADS)
    v = split_heads(v, MEM_HEADS)
    s = jnp.einsum('bhtd,bhmd->bhtm', q, k).astype(jnp.float32) * (MEM_HD ** -0.5)
    p = jax.nn.softmax(s, axis=-1).astype(v.dtype)
    return merge_heads(jnp.einsum('bhtm,bhmd->bhtd', p, v))

def stick_breaking_attention(q, k, v):
    seq = q.shape[2]
    scale = SB_HD ** -0.5
    outs = []
    for blk in range(seq // SB_BLOCK):
        t0 = blk * SB_BLOCK
        t1 = t0 + SB_BLOCK
        qb = q[:, :, t0:t1]
        kb = k[:, :, :t1]
        vb = v[:, :, :t1]
        z = jnp.einsum('bhtd,bhsd->bhts', qb, kb).astype(jnp.float32) * scale
        strict = jnp.arange(t1)[None, :] < jnp.arange(t0, t1)[:, None]
        log_stay = jnp.where(strict, jax.nn.log_sigmoid(-z), 0.0)
        later = lax.cumsum(log_stay, axis=3, reverse=True) - log_stay
        w = jnp.where(strict, jnp.exp(jax.nn.log_sigmoid(z) + later), 0.0)
        outs.append(jnp.einsum('bhts,bhsd->bhtd', w.astype(vb.dtype), vb))
    return jnp.concatenate(outs, axis=2)

def hgrn2_recurrence(q, k, v, log_f):
    b, h, s, dk = q.shape
    dv = v.shape[-1]
    nc = s // HG_CHUNK

    def chunks(t):
        return t.reshape(b, h, nc, HG_CHUNK, t.shape[-1]).transpose(2, 0, 1, 3, 4)

    causal = jnp.tril(jnp.ones((HG_CHUNK, HG_CHUNK), dtype=bool))[:, :, None]

    def step(state, inp):
        qc, kc, vc, gc = inp
        G = jnp.cumsum(gc.astype(jnp.float32), axis=2)
        G_last = G[:, :, -1:]
        o_inter = jnp.einsum('bhck,bhkv->bhcv', qc * jnp.exp(G), state)
        decay = jnp.exp(jnp.where(causal, G[:, :, :, None, :] - G[:, :, None, :, :], -jnp.inf))
        scores = jnp.einsum('bhtk,bhsk,bhtsk->bhts', qc, kc, decay)
        o_intra = jnp.einsum('bhts,bhsv->bhtv', scores, vc)
        k_dec = kc * jnp.exp(G_last - G)
        new_state = jnp.exp(G_last[:, :, 0])[..., None] * state + jnp.einsum('bhck,bhcv->bhkv', k_dec, vc)
        return new_state, o_inter + o_intra

    state0 = jnp.zeros((b, h, dk, dv), jnp.float32)
    _, o = lax.scan(step, state0, (chunks(q), chunks(k), chunks(v), chunks(log_f)))
    return o.transpose(1, 2, 0, 3, 4).reshape(b, h, s, dv)

def hgrn2_mixer(proj, lb, gnorm_g):
    wk = HG_HEADS * HG_DK
    wv = HG_HEADS * HG_DV
    q = proj[..., :wk]
    f_pre = proj[..., wk:2 * wk].astype(jnp.float32)
    i = proj[..., 2 * wk:2 * wk + wv]
    gate = proj[..., 2 * wk + wv:]
    log_f = jnp.logaddexp(jnp.log(lb), jnp.log1p(-lb) + jax.nn.log_sigmoid(f_pre))
    k = ((1.0 - lb) * jax.nn.sigmoid(-f_pre)).astype(q.dtype)
    o = hgrn2_recurrence(split_heads(q, HG_HEADS), split_heads(k, HG_HEADS),
                         split_heads(i, HG_HEADS), split_heads(log_f, HG_HEADS))
    of = o.astype(jnp.float32)
    of = of * lax.rsqrt(jnp.mean(jnp.square(of), axis=-1, keepdims=True) + RMS_EPS)
    o = merge_heads(of) * gnorm_g
    return (o * jax.nn.silu(gate.astype(jnp.float32))).astype(proj.dtype)

def hgrn2_lower_bounds(lower_bounds):
    p = jax.nn.softmax(lower_bounds.astype(jnp.float32), axis=0)
    return jnp.cumsum(p, axis=0) - p[0:1]

def second_inputs(seed: int = 0) -> dict:
    key = jax.random.key(seed)
    ks = jax.random.split(key, 16)
    d_hg = HG_HEADS * HG_DK
    nrm = jax.random.normal
    return {
        "x": nrm(ks[0], (BATCH, SEQ, D_MODEL), jnp.float32),
        "mem": nrm(ks[1], (BATCH, N_MEM, D_MODEL), jnp.float32),
        "w_in_sb": nrm(ks[2], (N_LAYERS_A, D_MODEL, SB_PROJ), jnp.float32) * D_MODEL ** -0.5,
        "w_in_hg": nrm(ks[3], (N_LAYERS_B, D_MODEL, HG_PROJ), jnp.float32) * D_MODEL ** -0.5,
        "w_mem_kv": nrm(ks[4], (DEPTH, D_MODEL, 2 * MEM_HEADS * MEM_HD), jnp.float32) * D_MODEL ** -0.5,
        "lower_bounds": 1.0 + 0.1 * nrm(ks[5], (DEPTH, d_hg), jnp.float32),
        "hg_norm_g": 1.0 + 0.05 * nrm(ks[6], (N_LAYERS_B, HG_HEADS * HG_DV), jnp.float32),
        "w_out": nrm(ks[7], (DEPTH, D_MIX, D_MODEL), jnp.float32) * (D_MIX ** -0.5 * DN_BETA),
        "ln_mix_g": 1.0 + 0.05 * nrm(ks[8], (DEPTH, D_MODEL), jnp.float32),
        "ln_mix_b": 0.02 * nrm(ks[9], (DEPTH, D_MODEL), jnp.float32),
        "w_up": nrm(ks[10], (DEPTH, D_MODEL, D_FF_2), jnp.float32) * D_MODEL ** -0.5,
        "w_down": nrm(ks[11], (DEPTH, D_FF_2, D_MODEL), jnp.float32) * (D_FF_2 ** -0.5 * DN_BETA),
        "ln_ffn_g": 1.0 + 0.05 * nrm(ks[12], (DEPTH, D_MODEL), jnp.float32),
        "ln_ffn_b": 0.02 * nrm(ks[13], (DEPTH, D_MODEL), jnp.float32),
    }

def second_block(x, mem, w_in_sb, w_in_hg, w_mem_kv, lower_bounds, hg_norm_g, w_out,
              ln_mix_g, ln_mix_b, w_up, w_down, ln_ffn_g, ln_ffn_b):
    lbs = hgrn2_lower_bounds(lower_bounds)
    w_sb = SB_HEADS * SB_HD
    for layer in range(DEPTH):
        slot = layer // N_MIXERS
        if layer % N_MIXERS == 0:
            proj = x @ w_in_sb[slot]
            q = split_heads(proj[..., :w_sb], SB_HEADS)
            k = split_heads(proj[..., w_sb:2 * w_sb], SB_HEADS)
            v = split_heads(proj[..., 2 * w_sb:3 * w_sb], SB_HEADS)
            q_mem = proj[..., 3 * w_sb:]
            mix = merge_heads(stick_breaking_attention(q, k, v))
        else:
            proj = x @ w_in_hg[slot]
            split = 2 * HG_HEADS * HG_DK + 2 * HG_HEADS * HG_DV
            q_mem = proj[..., split:]
            mix = hgrn2_mixer(proj[..., :split], lbs[layer], hg_norm_g[slot])
        mem_out = memory_attention(q_mem, mem, w_mem_kv[layer])
        y = jnp.concatenate([mix, mem_out.astype(mix.dtype)], axis=-1) @ w_out[layer]
        x = layer_norm(DN_ALPHA * x + y, ln_mix_g[layer], ln_mix_b[layer])
        h = jnp.square(jax.nn.relu(x @ w_up[layer]))
        x = layer_norm(DN_ALPHA * x + h @ w_down[layer], ln_ffn_g[layer], ln_ffn_b[layer])
    return x


def setup_inputs(seed=0):
    out = dict(first_inputs(seed))
    for name, value in second_inputs(seed + 1).items():
        if name != "x":
            out[name + "_2"] = value
    return out


def reference(
    x, c, w_ada, b_ada, norm1_g, w_in, rwkv_mu, rwkv_w0, rwkv_w_up, rwkv_a0, rwkv_a_up,
    rwkv_g_up, rwkv_k_k, rwkv_k_a, rwkv_r_k, rwkv_ln_g, rwkv_ln_b, q_norm_g, k_norm_g, w_out,
    norm2_g, w_router, b_router, w_gate_up, b_gate_up, w_down, b_down, mem_2, w_in_sb_2,
    w_in_hg_2, w_mem_kv_2, lower_bounds_2, hg_norm_g_2, w_out_2, ln_mix_g_2, ln_mix_b_2, w_up_2,
    w_down_2, ln_ffn_g_2, ln_ffn_b_2,
):
    x = first_block(
        x, c, w_ada, b_ada, norm1_g, w_in, rwkv_mu, rwkv_w0, rwkv_w_up, rwkv_a0, rwkv_a_up,
        rwkv_g_up, rwkv_k_k, rwkv_k_a, rwkv_r_k, rwkv_ln_g, rwkv_ln_b, q_norm_g, k_norm_g,
        w_out, norm2_g, w_router, b_router, w_gate_up, b_gate_up, w_down, b_down,
    )
    return second_block(
        x, mem_2, w_in_sb_2, w_in_hg_2, w_mem_kv_2, lower_bounds_2, hg_norm_g_2, w_out_2,
        ln_mix_g_2, ln_mix_b_2, w_up_2, w_down_2, ln_ffn_g_2, ln_ffn_b_2,
    )


_drawn_inputs = setup_inputs


def setup_inputs(seed=0):
    import zlib

    import numpy as np

    out = dict(_drawn_inputs(seed))
    spreads = {}
    factors = {'norm1_g': 3.438,
     'rwkv_w_up': 8.0,
     'rwkv_k_k': 25.269,
     'rwkv_k_a': 3.539,
     'rwkv_ln_g': 18.589,
     'rwkv_ln_b': 45.591,
     'q_norm_g': 8.0,
     'k_norm_g': 8.0,
     'b_router': 30.878,
     'b_gate_up': 62.231,
     'b_down': 64.0,
     'ln_ffn_b_2': 2.782,
     'norm2_g': 4.894}
    for name, (base, spread) in spreads.items():
        noise = np.random.default_rng([zlib.crc32(name.encode()), seed]).standard_normal(out[name].shape)
        drawn = base * np.exp(spread * noise) if base else spread * noise
        out[name] = __import__('jax').numpy.asarray(drawn.astype(out[name].dtype))
    for name, factor in factors.items():
        out[name] = (out[name] * factor).astype(out[name].dtype)
    return out
```

```python
from contextlib import ExitStack
import math

import numpy as np
import concourse.bass as bass
from concourse import mybir

F32 = mybir.dt.float32
I32 = mybir.dt.int32
ALU = mybir.AluOpType
ACT = mybir.ActivationFunctionType
AX = mybir.AxisListType

P = 128
D = 1024
T = 256
KT = D // P
TT = T // P
HD = 64
RW = 512
RT = RW // P
LOW, GLOW = 64, 160
LORA = 2 * LOW + GLOW
E_N = 32
FF = 1024
SB_W = 768
FF2 = 4096
BIG = -1.0e30
EXP_HALF = math.exp(-0.5)
ATT_SCALE = HD ** -0.5
ALPHA = 2.0 ** 0.25
CAP = 64
RING = 8
PRO_RING = 4
SLOT = 4096
UNROLL = 4
CHUNKS_E = 6
N_MOE = E_N * CHUNKS_E
TOP_K = 4
N_ITEM = E_N + (T * TOP_K - 1) // CAP + 1
N_PRO = 21
N_POST = 24
LEVELS = [1, 2, 4, 8, 16, 32, 64]

ROW = {}
_r = 0
for _name, _n in [("b_ada", 48), ("c", 8), ("norm1_g", 8), ("norm2_g", 8), ("mu", 15), ("w0", 4), ("a0", 4),
                  ("k_k", 4), ("k_a", 4), ("r_k", 4), ("ln_g", 4), ("ln_b", 4), ("qn", 1), ("kn", 1)]:
    ROW[_name] = _r
    _r += _n
N_ROWS = _r
ROW2 = {"lnm_g": N_ROWS, "lnm_b": N_ROWS + 8, "lnf_g": N_ROWS + 16, "lnf_b": N_ROWS + 24}
N_ROWS2 = 32

MILESTONES = {
    "tensor": [
        "par_turned", "xss", "lora_w", "lora_a", "lora_g", "kkss", "vturned", "qkss", "bonss",
        "biki_turned", "gn_mean", "gn_var", "x2ss", "logits", "ranks", "wt_turned",
    ],
    "scalar": [
        "sigc_ready", "h_ready", "tanh_ready", "gate_sig", "sg_ready", "a_ready", "kksq",
        "g_copied", "kk_norm", "qksq", "decays", "fac_ready", "vtok_ready", "qk_rs", "biki_tok",
        "gn_meanc", "gn_sq", "gn_rs", "x2sq", "h2_ready", "prob_e",
    ],
    "vector": [
        "eps_ready", "xsq_d", "silc_ready", "mods_ready", "kk_raw", "q_ready", "fac_arg",
        "kk_ready", "rk_ready", "biki_ready", "qk_ready", "bonus_ready", "gn_cent", "y_ready",
        "x2_ready", "sel_mask", "wt_ready", "npass_ready", "zeroed",
        "wtT_ready", "x3_ready",
    ],
}


class Chain:

    def __init__(self, eng, sem):
        self.eng, self.sem, self.n = eng, sem, 0

    def add(self, ins):
        self.n += 1
        ins.then_inc(self.sem, 1)

    def wait(self):
        self.eng.wait_ge(self.sem, self.n)

    def link(self, ins):
        self.add(ins)
        self.wait()


def build(nc, a, out):
    ctx = ExitStack()
    with ctx:
        def sb(name, shape, dt=F32):
            return ctx.enter_context(nc.sbuf_tensor(name, shape, dt))

        sems = {}

        def S(name):
            if name not in sems:
                sems[name] = ctx.enter_context(nc.semaphore(name))
            return sems[name]

        passed = {e: 0 for e in MILESTONES}

        def mark(name):
            e = next(e for e in MILESTONES if name in MILESTONES[e])
            assert MILESTONES[e][passed[e]] == name, (e, name)
            passed[e] += 1
            return S(f"{e}_milestones"), 1

        def at(name):
            e = next(e for e in MILESTONES if name in MILESTONES[e])
            return S(f"{e}_milestones"), MILESTONES[e].index(name) + 1

        ring = sb("ring", [P, RING, SLOT])
        ident = sb("ident", [P, P])
        ones = sb("ones", [P, P])
        blk = sb("blk", [P, P])
        rev_tri = sb("rev_tri", [P, P])
        pos_tri = sb("pos_tri", [P, P])
        iota = sb("iota", [P, T])
        alibi = sb("alibi", [P, 3 * P])
        sb_mask = sb("sb_mask", [P, 3 * P])
        sb_neg = sb("sb_neg", [P, 3 * P])
        mask_b = sb("mask_b", [P, 2 * P])
        mask_k = sb("mask_k", [P, 2 * P])
        lvl = sb("lvl", [P, len(LEVELS), P])
        lvl0n = sb("lvl0n", [P, P])
        par = sb("par", [P, N_ROWS + N_ROWS2])
        b_rout = sb("b_rout", [1, E_N])
        w_rout = sb("w_rout", [P, KT, E_N])
        mods = sb("mods", [P, 48])
        sc1 = sb("sc1", [P, KT])
        sc2 = sb("sc2", [P, KT])
        sigc = sb("sigc", [P, KT])
        rstd = sb("rstd", [P, T])
        small = sb("small", [P, 64])
        qmid = sb("qmid", [P, RT * TT])
        fac = sb("fac", [P, RT])
        logit = sb("logit", [P, TT, E_N])
        prob = sb("prob", [P, TT, E_N])
        wt = sb("wt", [P, TT, E_N])
        selm = sb("selm", [P, TT, E_N])
        posm = sb("posm", [P, TT, E_N])
        top8 = sb("top8", [P, TT, 8])
        cnt = sb("cnt", [1, 4, E_N])
        npass = sb("npass", [1, E_N], I32)
        cum = sb("cum", [1, E_N], I32)
        last_pass = sb("last_pass", [1, E_N], I32)
        item_f = sb("item_f", [1, N_ITEM])
        item_e = sb("item_e", [1, N_ITEM], I32)
        item_p = sb("item_p", [1, N_ITEM], I32)
        xT = sb("xT", [P, KT, T])
        hT = sb("hT", [P, KT, T])
        tok = sb("tok", [P, TT, D])
        yT = sb("yT", [P, KT, T])
        work = sb("work", [P, 6560])
        psum = ctx.enter_context(nc.psum_tensor("psum", [P, 8, 512], F32))

        def B(i):
            return psum[:, i, :]

        ws = ring[:, PRO_RING:RING, :].rearrange("p a b -> p (a b)")

        def view(base, off, shape):
            n = int(np.prod(shape))
            v = base[:, off:off + n]
            if len(shape) == 1:
                return v
            names = "abcd"[:len(shape)]
            kw = {names[i]: shape[i] for i in range(len(shape))}
            return v.rearrange(f"p ({' '.join(names)}) -> p {' '.join(names)}", **kw)

        hT_f = hT[:, :, :].rearrange("p a b -> p (a b)")
        tok_f = tok[:, :, :].rearrange("p a b -> p (a b)")
        work_f = work[:, :]

        mix = view(ws, 0, [12, T])
        r_m, k_m, v_m = mix[:, 0:4, :], mix[:, 4:8, :], mix[:, 8:12, :]
        lo = view(ws, 3072, [3, T])
        vtok = view(ws, 3840, [TT, RW])
        kr = view(ws, 4864, [RT, TT, 2, P])
        bi = view(ws, 6912, [RT, TT, P])
        ki = view(ws, 7936, [RT, TT, P])
        bitok = view(ws, 8960, [RW])
        kitok = view(ws, 9472, [RW])
        aT = view(ws, 9984, [RT, T])
        gT = view(ws, 11008, [RT, T])
        q_cum = view(ws, 12032, [RT, T])
        sg = view(ws, 13056, [RT, T])
        kk = view(ws, 14080, [RT, T])
        k2 = view(ws, 15104, [RT, T])
        praw = [view(work_f, 0, [4, T + 1]), view(work_f, 1028, [4, T + 1])]
        qk = view(work_f, 2056, [8, T])
        vm = view(work_f, 4104, [TT, RW])
        s0 = view(work_f, 5128, [RT, HD])
        bonus = view(work_f, 5384, [RT, T])
        atr = view(work_f, 0, [4, 2 * P])
        ktr = view(work_f, 1028, [4, 2 * P])
        sc_p = view(hT_f, 0, [2, 3 * P])
        pt_p = view(hT_f, 768, [2, 3 * P])
        x_inv, xt_inv, y_inv = view(tok_f, 0, [4, P]), view(tok_f, 512, [4, P]), view(tok_f, 1024, [4, P])
        bt = [view(tok_f, 1536, [4, P]), view(hT_f, 1536, [4, P])]
        rr, w1, w2, uu = (view(ws, 9984 + 256 * i, [4, HD]) for i in range(4))
        prow = view(ws, 0, [P])
        prow2 = view(ws, 128, [P])
        wl = view(work_f, 2056, [3, RW])

        b_down = view(work_f, 0, [D])[0:E_N, :]

        silc = view(work_f, 5384, [KT, 32])
        ada_sb = [view(ws, 8192 + 512 * i, [512]) for i in range(2)]

        act = view(work_f, 2048, [4, 2, CAP])
        act_tm = view(work_f, 2560, [512])
        xe = view(work_f, 3072, [4, 2, CAP])
        ended = yT[0:1, 2:8, :].rearrange("p a b -> p (a b)").rearrange("p (g e) -> p g e", g=N_ITEM)
        x_tm = yT[:, 0:2, :].rearrange("p a b -> p (a b)")
        ye = view(work_f, 3584, [512])
        sel = view(work_f, 4096, [TT, CAP])
        selw = view(work_f, 4224, [TT, 2, CAP])
        selT = view(work_f, 4480, [T])
        gt = view(work_f, 4736, [512])
        ut = view(work_f, 5248, [512])
        sgm = view(work_f, 5760, [512])
        one_e = view(work_f, 6272, [CAP])[0:E_N, :]
        bgu = hT_f[0:E_N, :]

        sbq = view(ws, 0, [12, T])
        sbv = view(ws, 3072, [TT, SB_W])
        qm = view(ws, 4608, [2, T])
        km = view(ws, 5120, [2, T])
        vmem = view(ws, 5632, [TT, T])
        memT = view(ws, 6144, [KT, T])
        zs = view(ws, 8192, [2, 3 * P])
        ee = view(ws, 8960, [2, 3 * P])
        sp = view(ws, 9728, [2, 3 * P])
        dd = view(ws, 10496, [2, 3 * P])
        ms = view(ws, 11264, [2, 2, T])
        mpt = view(ws, 12288, [2, 2, T])
        hid = view(ws, 0, [32, T])
        fr = view(ws, 8192, [2, 2, T])

        def bank2(i):
            return B(i).rearrange("p (a b) -> p a b", a=2)

        def chunk_cols(w, c0, n):
            return w[:, c0:c0 + n].rearrange("(k p) n -> p k n", p=P)

        W_IN = [(1536, LORA), (512, 512), (0, 512), (1024, 512), (1824, 512), (2336, 512), (2848, 512)]

        def pro_slot(n):
            return (n + 3) % PRO_RING

        def slot8(s, n=512):
            return ring[:, s, 0:KT * n].rearrange("p (k n) -> p k n", k=KT)

        def moe_slot(m):
            return (m + PRO_RING) % RING

        block = ctx.enter_context(nc.Block())

        @block.sync
        def _(sp_):
            def load(dst, src, sem):
                nc.sync.dma_start(dst, src).then_inc(sem, 16)

            for n in range(N_PRO):
                if n >= PRO_RING:
                    sp_.wait_ge(S("halves_used"), 2 * (n - PRO_RING + 1))
                s = pro_slot(n)
                if n < 12:
                    load(slot8(s), chunk_cols(a["w_ada"][0], 512 * n, 512), S(f"pro_in{s}"))
                elif n < 19:
                    c0, w = W_IN[n - 12]
                    load(slot8(s, w), chunk_cols(a["w_in"][0], c0, w), S(f"pro_in{s}"))
                else:
                    load(slot8(s), chunk_cols(a["w_out"][0], 512 * (n - 19), 512), S(f"pro_in{s}"))

            def moe_src(e, j):
                if j < 4:
                    c0 = FF * (j // 2) + 512 * (j % 2)
                    return a["w_gate_up"][0, e, :, c0:c0 + 512].rearrange("(k p) n -> p k n", p=P)
                return a["w_down"][0, e, 512 * (j - 4):512 * (j - 3), :].rearrange("(k p) n -> p k n", p=P)

            def moe_src_dyn(e, j):
                if j < 4:
                    c0 = FF * (j // 2) + 512 * (j % 2)
                    return a["w_gate_up"][0, bass.ds(e, 1), :, c0:c0 + 512].rearrange("o (k p) n -> p (o k) n", p=P)
                return a["w_down"][0, bass.ds(e, 1), 512 * (j - 4):512 * (j - 3), :].rearrange(
                    "o (k p) n -> p (o k) n", p=P)

            def moe_dst(m):
                s, j = moe_slot(m), m % CHUNKS_E
                return ring[:, s, :].rearrange("p (k n) -> p k n", k=KT if j < 4 else 4)

            sp_.wait_ge(S("work_space_free"), 1)
            for m in range(RING):
                if m >= PRO_RING:
                    sp_.wait_ge(S("halves_used"), 2 * (N_PRO - PRO_RING + (m - PRO_RING) + 1))
                load(moe_dst(m), moe_src(m // CHUNKS_E, m % CHUNKS_E), S(f"moe_in{moe_slot(m)}"))
            sp_.wait_ge(*at("npass_ready"))

            def freed(j, g):
                if j < 4:
                    sp_.wait_ge(S("e_gu"), g * 2 + (1 if j < 2 else 2))
                else:
                    sp_.wait_ge(S("e_down"), g + 1)

            def last_of(e):
                return sp_.value_load(last_pass[0:1, bass.ds(e, 1)], min_val=0, max_val=N_ITEM - 2)

            step = UNROLL * CHUNKS_E
            full = (N_MOE - RING) // step
            with sp_.Fori(0, full) as i:
                for c in range(step):
                    m = RING + c
                    if c % CHUNKS_E == 0:
                        g = last_of(i * UNROLL + c // CHUNKS_E)
                    freed(c % CHUNKS_E, g)
                    load(moe_dst(m), moe_src_dyn(i * UNROLL + m // CHUNKS_E, m % CHUNKS_E),
                         S(f"moe_in{moe_slot(m)}"))
            for c in range(full * step, N_MOE - RING):
                m = RING + c
                if c % CHUNKS_E == 0:
                    g = last_of(c // CHUNKS_E)
                freed(c % CHUNKS_E, g)
                load(moe_dst(m), moe_src(m // CHUNKS_E, m % CHUNKS_E), S(f"moe_in{moe_slot(m)}"))
            g = last_of(E_N - 1)

            for n in range(N_POST):
                s = n % PRO_RING
                if n < PRO_RING:
                    freed(CHUNKS_E - PRO_RING + n, g)
                else:
                    sp_.wait_ge(S("halves_used"), 2 * (N_PRO + n - PRO_RING + 1))
                if n < 5:
                    src, dst = chunk_cols(a["w_in_sb_2"][0], 512 * n, 512), slot8(s)
                elif n == 5:
                    src, dst = chunk_cols(a["w_mem_kv_2"][0], 0, 512), slot8(s)
                elif n < 8:
                    src, dst = chunk_cols(a["w_out_2"][0], 512 * (n - 6), 512), slot8(s)
                elif n < 16:
                    src, dst = chunk_cols(a["w_up_2"][0], 512 * (n - 8), 512), slot8(s)
                else:
                    r0 = 512 * (n - 16)
                    src = a["w_down_2"][0, r0:r0 + 512, :].rearrange("(k p) n -> p k n", p=P)
                    dst = ring[:, s, :].rearrange("p (k n) -> p k n", k=4)
                load(dst, src, S(f"post_in{s}"))
            sp_.wait_ge(S("out_ready_a"), 2)
            sp_.wait_ge(S("out_ready_d"), 2)
            nc.sync.dma_start(out[0].rearrange("(i p) d -> p i d", p=P), tok[:, :, :]).then_inc(S("out_stored"), 16)
            sp_.wait_ge(S("out_stored"), 16)

        @block.gpsimd
        def _(g):
            ch = Chain(g, S("pool_chain"))
            g_ = nc.gpsimd
            g_.memset(prow, 0.0).then_inc(S("prow_zero"), 1)
            ch.link(g_.memset(ident[:, :], 0.0))
            ch.link(g_.memset(ones[:, :], 1.0))
            ch.link(g_.memset(blk[:, :], 0.0))
            ch.link(g_.memset(rev_tri[:, :], 1.0))
            ch.link(g_.memset(pos_tri[:, :], 1.0))
            ch.link(g_.memset(lvl[:, :, :], 0.0))
            ch.link(g_.memset(lvl0n[:, :], 0.0))
            ch.link(g_.memset(mask_b[:, 0:P], 1.0))
            ch.link(g_.memset(mask_b[:, P:2 * P], -1.0))
            ch.link(g_.memset(mask_k[:, :], 1.0))
            ch.link(g_.memset(sb_mask[:, :], 1.0))
            ch.link(g_.memset(sb_neg[:, :], 0.0))
            for b in range(2):
                ch.link(g_.memset(praw[b][:, :, 0:1], 0.0))
            ch.wait()

            def select(v, pattern, base, mult, op, fill=0.0):
                ch.link(g_.affine_select(out=v, in_=v, pattern=pattern, base=base, channel_multiplier=mult,
                                        compare_op=op, fill=fill))

            select(ident[:, :], [[-1, P]], 0, 1, ALU.not_equal, 1.0)
            ch.link(g_.memset(blk[0:HD, 0:HD], 1.0))
            ch.link(g_.memset(blk[HD:P, HD:P], 1.0))
            select(rev_tri[:, :], [[-1, P]], 0, 1, ALU.is_ge)
            select(pos_tri[:, :], [[1, P]], 0, -1, ALU.is_gt)
            for m in (mask_b, mask_k):
                select(m[:, 0:P], [[1, P]], 0, -1, ALU.is_gt)
                select(m[:, P:2 * P], [[1, P]], 0, -1, ALU.is_ge)
            select(sb_mask[:, 0:T], [[1, T]], 0, -1, ALU.is_gt)
            select(sb_mask[:, T:3 * P], [[1, P]], 0, -1, ALU.is_gt)
            select(sb_neg[:, 0:T], [[1, T]], 0, -1, ALU.is_gt, BIG)
            select(sb_neg[:, T:3 * P], [[1, P]], 0, -1, ALU.is_gt, BIG)
            ch.link(g_.iota(iota[:, :], pattern=[[1, T]], base=0, channel_multiplier=0,
                           allow_small_or_imprecise_dtypes=True))
            ch.link(g_.iota(alibi[:, 0:P], pattern=[[1, P]], base=0, channel_multiplier=-1,
                           allow_small_or_imprecise_dtypes=True))
            ch.link(g_.iota(alibi[:, P:3 * P], pattern=[[1, T]], base=-P, channel_multiplier=-1,
                           allow_small_or_imprecise_dtypes=True))
            for n, b in enumerate(LEVELS):
                v = lvl[:, n, :].rearrange("p (j x) -> p j x", x=2 * b)[:, :, b:2 * b]
                ch.link(g_.memset(v, -1.0 if n == 0 else 1.0))
            ch.link(g_.memset(lvl0n[:, :].rearrange("p (j x) -> p j x", x=2)[:, :, 0:1], -1.0))
            ch.wait()
            select(alibi[:, 0:P], [[-1, P]], 0, 1, ALU.is_ge, BIG)
            select(alibi[:, P:3 * P], [[-1, T]], P, 1, ALU.is_ge, BIG)
            for n, b in enumerate(LEVELS):
                v = lvl[:, n, :].rearrange("p (j x) -> p j x", x=2 * b)[:, :, b:2 * b]
                select(v, [[-2 * b, P // (2 * b)], [0, b]], 0, 1, ALU.is_ge)
            v = lvl0n[:, :].rearrange("p (j x) -> p j x", x=2)[:, :, 0:1]
            select(v, [[-2, HD], [0, 1]], -1, 1, ALU.is_equal)
            ch.wait()
            for n, b in enumerate(LEVELS):
                v = lvl[:, n, :].rearrange("p (j x) -> p j x", x=2 * b)[:, :, b:2 * b]
                last = g_.affine_select(out=v, in_=v, pattern=[[2 * b, P // (2 * b)], [0, b]], base=b - 1,
                                        channel_multiplier=-1, compare_op=ALU.is_ge, fill=0.0)
                if n < len(LEVELS) - 1:
                    ch.link(last)
            last.then_inc(S("consts"), 1)

            for gi in range(4):
                for l in range(1, 7):
                    n = 6 * gi + l - 1
                    if l == 1:
                        g.wait_ge(S("atr_ready"), gi + 1)
                    if n >= 2:
                        g.wait_ge(S("bt_used"), n - 1)
                    g_.tensor_tensor(bt[n % 2], atr[:, :, 0:P], lvl[:, l:l + 1, :].broadcast_to([P, 4, P]),
                                     ALU.mult).then_inc(S("bt_ready"), 1)

        @block.tensor
        def _(pe):
            mm = nc.tensor.matmul

            def tr(o, i, n=P):
                return nc.tensor.transpose(o, i, ident[0:n, 0:n])

            pe.wait_ge(S("consts"), 1)
            pe.wait_ge(S("x_in"), 16)
            for b in range(4):
                for k in (2 * b, 2 * b + 1):
                    for i in range(TT):
                        last = tr(bank2(4 + b)[:, k % 2, i * P:(i + 1) * P], tok[:, i, k * P:(k + 1) * P])
                last.then_inc(S("x_turned"), 1)
            pe.wait_ge(S("par_in"), 16 * N_PAR_DMA)
            tr(B(1)[:, 0:N_ROWS], prow[0:N_ROWS, :], N_ROWS)
            last = tr(B(1)[:, N_ROWS:N_ROWS + N_ROWS2], prow2[0:N_ROWS2, :], N_ROWS2)
            last.then_inc(*mark("par_turned"))
            pe.wait_ge(S("xsq_a"), 2)
            pe.wait_ge(*at("xsq_d"))
            for k in range(KT):
                last = mm(B(3)[:, 0:T], ones[:, :], hT[:, k, :], start=k == 0, stop=k == KT - 1)
            last.then_inc(*mark("xss"))

            def arrived(n):
                pe.wait_ge(S(f"pro_in{pro_slot(n)}"), 16 * (sum(pro_slot(x) == pro_slot(n) for x in range(n + 1))))

            pe.wait_ge(*at("silc_ready"))
            for n in range(13):
                if n < 12:
                    arrived(n)
                    if n >= 2:
                        pe.wait_ge(S("ada_copied"), n - 1)
                    w = slot8(pro_slot(n))
                    for k in range(KT):
                        q = 32 * (k % 4)
                        last = mm(B([0, 4][n % 2])[q:q + 32, :], silc[:, k, :], w[:, k, :], start=k < 4, stop=k >= 4)
                        if k % 4 == 3:
                            last.then_inc(S("halves_used"), 1)
                if n >= 1:
                    m = n - 1
                    pe.wait_ge(S("ada_copied"), m + 1)
                    if m >= 2:
                        pe.wait_ge(S("ada_summed"), m - 1)
                    for j in range(4):
                        last = tr(B(5 + m % 2)[:, j * P:(j + 1) * P], ada_sb[m % 2][:, j * P:(j + 1) * P])
                    last.then_inc(S("ada_turned"), 1)

            def proj(n, job):
                arrived(n)
                w0 = W_IN[n - 12][1]
                w = slot8(pro_slot(n), w0)
                for half in range(2):
                    if job >= 4:
                        pe.wait_ge(S("proj_copied"), job - 3)
                    bank = 1 + job % 4
                    if n == 18:
                        for k in range(KT):
                            last = mm(B(bank), hT[:, k, half * P:(half + 1) * P], w[:, k, :],
                                      start=k == 0, stop=k == KT - 1)
                    else:
                        for jj in range(2):
                            j = 2 * half + jj
                            m = min(P, w0 - j * P)
                            if m <= 0:
                                continue
                            for k in range(KT):
                                last = mm(bank2(bank)[0:m, jj, :], w[:, k, j * P:j * P + m], hT[:, k, :],
                                          start=k == 0, stop=k == KT - 1)
                    last.then_inc(S("halves_used"), 1)
                    job += 1
                return job

            pe.wait_ge(*at("h_ready"))
            job = 0
            for n in (12, 13, 14):
                job = proj(n, job)
            pe.wait_ge(S("wl_in"), 16 * 4)
            pe.wait_ge(*at("tanh_ready"))
            pe.wait_ge(S("xcopy_a"), 2)
            pe.wait_ge(S("xcopy_d"), 2)
            for m in range(RT):
                last = mm(bank2(5 + m // 2)[:, m % 2, :], wl[0:LOW, 0, m * P:(m + 1) * P], lo[0:LOW, 0, :],
                          start=True, stop=True)
            last.then_inc(*mark("lora_w"))
            pe.wait_ge(*at("mods_ready"))
            for m in range(RT):
                last = mm(bank2([7, 0][m // 2])[:, m % 2, :], wl[LOW:P, 0, m * P:(m + 1) * P], lo[LOW:P, 0, :],
                          start=True, stop=True)
            last.then_inc(*mark("lora_a"))
            job = proj(15, job)
            pe.wait_ge(*at("sg_ready"))
            pe.wait_ge(*at("gate_sig"))
            for m in range(RT):
                mm(bank2(5 + m // 2)[:, m % 2, :], wl[:, 1, m * P:(m + 1) * P], lo[:, 1, :], start=True, stop=False)
                last = mm(bank2(5 + m // 2)[:, m % 2, :], wl[0:GLOW - P, 2, m * P:(m + 1) * P], lo[0:GLOW - P, 2, :],
                          start=False, stop=True)
            last.then_inc(*mark("lora_g"))
            pe.wait_ge(*at("kksq"))
            pe.wait_ge(*at("a_ready"))
            kki = ki.rearrange("p m c t -> p (m c t)")
            mm(B(7), blk[:, :], kki[:, 0:512], start=True, stop=True)
            mm(B(0), blk[:, :], kki[:, 512:1024], start=True, stop=True).then_inc(*mark("kkss"))
            for n in (16, 17, 18):
                if n == 16:
                    pe.wait_ge(*at("g_copied"))
                job = proj(n, job)
            pe.wait_ge(S("mixed"), 4)
            for c in range(TT):
                for m in range(RT):
                    last = tr(B(5 + c)[:, m * P:(m + 1) * P], v_m[:, m, c * P:(c + 1) * P])
            last.then_inc(*mark("vturned"))
            pe.wait_ge(*at("qksq"))
            pe.wait_ge(S("proj_copied"), 14)
            for j in range(4):
                last = mm(B(1 + j), blk[:, :], tok_f[:, 512 * j:512 * (j + 1)], start=True, stop=True)
            last.then_inc(*mark("qkss"))
            pe.wait_ge(*at("rk_ready"))
            bon = bonus.rearrange("p m t -> p (m t)")
            mm(B(7), blk[:, :], bon[:, 0:512], start=True, stop=True)
            mm(B(0), blk[:, :], bon[:, 512:1024], start=True, stop=True).then_inc(*mark("bonss"))
            pe.wait_ge(*at("vtok_ready"))
            pe.wait_ge(*at("biki_ready"))
            for m in range(RT):
                tr(B(5)[:, m * P:(m + 1) * P], bi[:, m, 0, :])
            for m in range(RT):
                last = tr(B(6)[:, m * P:(m + 1) * P], ki[:, m, 0, :])
            last.then_inc(*mark("biki_turned"))
            pe.wait_ge(*at("biki_tok"))
            pe.wait_ge(*at("qk_ready"))
            pe.wait_ge(*at("bonus_ready"))

            def moba_scores(i):
                for par_ in range(2):
                    b, p0 = [(1, 2), (7, 0)][i % 2][par_], HD * par_
                    mm(B(b)[:, 0:P], qk[p0:p0 + HD, i, 0:P], qk[p0:p0 + HD, 4 + i, 0:P], start=True, stop=True)
                    last = mm(B(b)[:, P:3 * P], qk[p0:p0 + HD, i, P:T], qk[p0:p0 + HD, 4 + i, :],
                              start=True, stop=True)
                last.then_inc(S("moba_s"), 1)

            moba_scores(0)
            for i in range(RT):
                if i + 1 < RT:
                    moba_scores(i + 1)
                pe.wait_ge(S("moba_p"), i + 1)
                for par_ in range(2):
                    for j in range(3):
                        last = tr(B(3 + par_)[:, j * P:(j + 1) * P], sc_p[:, par_, j * P:(j + 1) * P])
                last.then_inc(S("moba_t"), 1)
                pe.wait_ge(S("moba_tc"), i + 1)
                for par_ in range(2):
                    h, p0 = 2 * i + par_, HD * par_
                    o = B(5 + i % 2)
                    mm(o[p0:p0 + HD, 0:T], vm[:, 0, h * HD:(h + 1) * HD], pt_p[:, par_, 0:T],
                       start=True, stop=False, skip_group_check=True)
                    last = mm(o[p0:p0 + HD, P:T], vm[:, 1, h * HD:(h + 1) * HD], pt_p[:, par_, T:3 * P],
                              start=False, stop=True, skip_group_check=True)
                last.then_inc(S("moba_o"), 1)

            pe.wait_ge(S("moba_oc"), RT)
            for gi in range(4):
                c, hh = gi // 2, gi % 2
                heads = [(q, q // 2, 2 * hh + q % 2, HD * (q // 2)) for q in range(4)]
                if gi:
                    pe.wait_ge(S("yo_copied"), gi)
                for q, par_, m, p0 in heads:
                    last = mm(B(par_)[:, (q % 2) * T:(q % 2 + 1) * T], bi[p0:p0 + HD, m, c, :],
                              kr[p0:p0 + HD, m, c, :, :].rearrange("p a b -> p (a b)"), start=True, stop=True)
                last.then_inc(S("grp_m"), 1)
                for q, par_, m, p0 in heads:
                    last = mm(B(4 + par_)[:, (q % 2) * P:(q % 2 + 1) * P], kr[p0:p0 + HD, m, c, 0, :],
                              bi[p0:p0 + HD, m, c, :], start=True, stop=True)
                last.then_inc(S("grp_m"), 1)
                for q, par_, m, p0 in heads:
                    last = mm(B(2 + par_)[:, (q % 2) * T:(q % 2 + 1) * T], ki[p0:p0 + HD, m, c, :],
                              kr[p0:p0 + HD, m, c, :, :].rearrange("p a b -> p (a b)"), start=True, stop=True)
                last.then_inc(S("grp_m"), 1)
                for l in range(1, 6):
                    n = 6 * gi + l - 1
                    pe.wait_ge(S("x_ready"), 6 * gi + l)
                    pe.wait_ge(S("xt_ready"), 6 * gi + l)
                    pe.wait_ge(S("bt_ready"), n + 1)
                    for q in range(4):
                        last = mm(B(6)[:, q * P:(q + 1) * P], bt[n % 2][:, q, :], x_inv[:, q, :], start=True, stop=True)
                    last.then_inc(S("bt_used"), 1)
                    pe.wait_ge(S("y_copied"), 5 * gi + l)
                    for q in range(4):
                        last = mm(B(4)[:, q * P:(q + 1) * P], y_inv[:, q, :], xt_inv[:, q, :], start=True, stop=True)
                    last.then_inc(S("xtp"), 1)
                    if l < 5:
                        for q in range(4):
                            last = mm(B(7)[:, q * P:(q + 1) * P], xt_inv[:, q, :], y_inv[:, q, :],
                                      start=True, stop=True)
                        last.then_inc(S("xp"), 1)
                pe.wait_ge(S("ktr_ready"), gi + 1)
                if c:
                    pe.wait_ge(S("s0_ready"), 2)
                for q, par_, m, p0 in heads:
                    h = 2 * m + par_
                    o = B(5 + par_)[:, (q % 2) * HD:(q % 2 + 1) * HD]
                    last = mm(o, ktr[:, q, 0:P], vtok[:, c, h * HD:(h + 1) * HD], start=True, stop=c == 0)
                    if c:
                        last = mm(o, kr[p0:p0 + HD, m, 1, 0, :], s0[p0:p0 + HD, m, :], start=False, stop=True)
                last.then_inc(S("r_done"), 1)
                pe.wait_ge(S("xt_ready"), 6 * gi + 6)
                pe.wait_ge(S("r_copied"), gi + 1)
                for q in range(4):
                    last = mm(B(7)[:, q * HD:(q + 1) * HD], xt_inv[:, q, :], rr[:, q, :], start=True, stop=True)
                last.then_inc(S("w_done"), 1)
                n = 6 * gi + 5
                pe.wait_ge(S("bt_ready"), n + 1)
                pe.wait_ge(S("w_copied"), 2 * gi + 1)
                for q in range(4):
                    last = mm(B(4)[:, q * HD:(q + 1) * HD], bt[n % 2][:, q, :], w1[:, q, :], start=True, stop=True)
                last.then_inc(S("bt_used"), 1)
                pe.wait_ge(S("w_copied"), 2 * gi + 2)
                for q in range(4):
                    last = mm(B(7)[:, q * HD:(q + 1) * HD], xt_inv[:, q, :], w2[:, q, :], start=True, stop=True)
                last.then_inc(S("w_done"), 1)
                pe.wait_ge(S("u_ready"), gi + 1)
                for q, par_, m, p0 in heads:
                    h = 2 * m + par_
                    o = B(5)[p0:p0 + HD, (q % 2) * P:(q % 2 + 1) * P]
                    mm(o, uu[:, q, :], atr[:, q, P:2 * P], start=True, stop=False)
                    last = mm(o, vtok[:, c, h * HD:(h + 1) * HD], ktr[:, q, P:2 * P], start=False, stop=c == 0)
                    if c:
                        last = mm(o, s0[p0:p0 + HD, m, :], kr[p0:p0 + HD, m, 1, 1, :], start=False, stop=True)
                last.then_inc(S("yo_done"), 1)
                if c == 0:
                    for q, par_, m, p0 in heads:
                        h = 2 * m + par_
                        o = B(6)[p0:p0 + HD, (q % 2) * HD:(q % 2 + 1) * HD]
                        mm(o, bitok[:, h * HD:(h + 1) * HD], uu[:, q, :], start=True, stop=False)
                        last = mm(o, kitok[:, h * HD:(h + 1) * HD], vtok[:, 0, h * HD:(h + 1) * HD],
                                  start=False, stop=True)
                    last.then_inc(S("send_done"), 1)
            yrf = yT[:, 0:RT, :].rearrange("p m t -> p (m t)")
            pe.wait_ge(S("yo_copied"), 4)
            for j in range(2):
                last = mm(B(j), blk[:, :], yrf[:, 512 * j:512 * (j + 1)], start=True, stop=True)
            last.then_inc(*mark("gn_mean"))
            pe.wait_ge(*at("gn_sq"))
            gsq = tok_f[:, 0:1024]
            for j in range(2):
                last = mm(B(2 + j), blk[:, :], gsq[:, 512 * j:512 * (j + 1)], start=True, stop=True)
            last.then_inc(*mark("gn_var"))

            pe.wait_ge(*at("y_ready"))
            for n in (19, 20):
                arrived(n)
                w = slot8(pro_slot(n))
                for half in range(2):
                    b = 4 + 2 * (n - 19) + half
                    for jj in range(2):
                        j = 2 * half + jj
                        for k in range(KT):
                            last = mm(bank2(b)[:, jj, :], w[:, k, j * P:(j + 1) * P], yT[:, k, :],
                                      start=k == 0, stop=k == KT - 1)
                    last.then_inc(S("halves_used"), 1)
            pe.wait_ge(*at("x2sq"))
            for k in range(KT):
                last = mm(B(0)[:, 0:T], ones[:, :], hT[:, k, :], start=k == 0, stop=k == KT - 1)
            last.then_inc(*mark("x2ss"))
            pe.wait_ge(*at("h2_ready"))
            pe.wait_ge(S("rout_in"), 32)
            for i in range(TT):
                o = B(1)[:, i * E_N:(i + 1) * E_N]
                for k in range(KT):
                    mm(o, hT[:, k, i * P:(i + 1) * P], w_rout[:, k, :], start=k == 0, stop=False)
                last = mm(o, ones[0:1, :], b_rout[0:1, :], start=False, stop=True)
            last.then_inc(*mark("logits"))
            for b in range(4):
                for jj in range(2):
                    for i in range(TT):
                        k = 2 * b + jj
                        last = tr(B(4 + b)[:, (i * 2 + jj) * P:(i * 2 + jj + 1) * P], hT[:, k, i * P:(i + 1) * P])
                last.then_inc(S("h2_turned"), 1)
            pe.wait_ge(*at("sel_mask"))
            mm(B(2)[:, 0:E_N], pos_tri[:, :], selm[:, 0, :], start=True, stop=True)
            mm(B(2)[:, E_N:2 * E_N], ones[:, :], selm[:, 0, :], start=True, stop=False)
            mm(B(2)[:, E_N:2 * E_N], pos_tri[:, :], selm[:, 1, :], start=False, stop=True)
            for i in range(TT):
                last = mm(B(3)[0:1, 0:E_N], ones[:, 0:1], selm[:, i, :], start=i == 0, stop=i == TT - 1)
            last.then_inc(*mark("ranks"))
            pe.wait_ge(*at("wt_ready"))
            for i in range(TT):
                last = tr(B(0)[0:E_N, i * P:(i + 1) * P], wt[:, i, :])
            last.then_inc(*mark("wt_turned"))
            pe.wait_ge(*at("wtT_ready"))
            pe.wait_ge(S("h2tok_a"), 2)
            pe.wait_ge(S("h2tok_d"), 2)
            pe.wait_ge(S("b_down_in"), 16)
            for m in range(KT):
                mm(bank2(4 + m // 2)[:, m % 2, :], b_down[:, m * P:(m + 1) * P], gt[0:E_N, 0:T],
                   start=m % 2 == 0, stop=False, skip_group_check=True)

            pe.wait_ge(S("bgu_in"), 16)
            def gather(g):
                pe.wait_ge(S("e_sel"), g)
                for ti in range(TT):
                    for h in range(2):
                        last = mm(B(0)[CAP * h:CAP * (h + 1), :], sel[:, ti, :],
                                  tok[:, ti, 512 * h:512 * (h + 1)], start=ti == 0, stop=ti == TT - 1)
                last.then_inc(S("e_gather"), 1)

            def turn_x(g):
                pe.wait_ge(S("e_xtm"), g)
                for c in range(4):
                    last = tr(B(0)[:, c * P:(c + 1) * P], x_tm[:, c * P:(c + 1) * P])
                last.then_inc(S("e_xturn"), 1)

            def scatter():
                for c in range(4):
                    for h in range(2):
                        m = 4 * h + c
                        last = mm(bank2(4 + m // 2)[:, m % 2, :], ye[CAP * h:CAP * (h + 1), c * P:(c + 1) * P],
                                  selT[CAP * h:CAP * (h + 1), :], start=False, stop=False,
                                  skip_group_check=True)
                return last

            gather(1)
            turn_x(1)
            pe.wait_ge(*at("npass_ready"))
            pg = pe.alloc_register("pe_pg")
            pe.reg_mov(pg, 0)
            with pe.Fori(0, E_N // UNROLL) as i:
                for j in range(UNROLL):
                    def landed(c):
                        m = CHUNKS_E * j + c
                        pe.wait_ge(S(f"moe_in{moe_slot(m)}"), i * (16 * 3) + 16 * (m // RING + 1))

                    slots = [moe_slot(CHUNKS_E * j + c) for c in range(CHUNKS_E)]
                    n = pe.value_load(npass[0:1, bass.ds(i * UNROLL + j, 1)], min_val=1, max_val=T // CAP)
                    with pe.Fori(0, n):
                        g = pe.snap(pg)
                        pe.reg_add(pg, pg, 1)
                        pe.wait_ge(S("e_one"), g + 1)
                        pe.wait_ge(S("e_xe"), g + 1)
                        pe.wait_ge(S("e_selT"), g + 1)
                        for u in range(2):
                            for h in range(2):
                                c0 = FF * u + 512 * h
                                mm(B(1 + u)[CAP * h:CAP * (h + 1), :], one_e, bgu[:, c0:c0 + 512],
                                   start=True, stop=False)
                            landed(2 * u)
                            landed(2 * u + 1)
                            for k in range(KT):
                                for h in range(2):
                                    w = slot8(slots[2 * u + h])
                                    last = mm(B(1 + u)[CAP * h:CAP * (h + 1), :], xe[:, k % 4, k // 4, :], w[:, k, :],
                                              start=False, stop=k == KT - 1)
                            last.then_inc(S("e_gu"), 1)
                            if u == 0:
                                pe.wait_ge(S("e_ye"), g + 1)
                                scatter()
                        gather(g + 2)
                        pe.wait_ge(S("e_act"), g + 1)
                        for c in range(4):
                            last = tr(B(3)[:, c * P:(c + 1) * P], act_tm[:, c * P:(c + 1) * P])
                        last.then_inc(S("e_actturn"), 1)
                        pe.wait_ge(S("e_selw"), g + 1)
                        for ti in range(TT):
                            last = tr(B(1)[:, ti * P:(ti + 1) * P], selw[:, ti, :, :].rearrange("p a b -> p (a b)"))
                        last.then_inc(S("e_selturn"), 1)
                        turn_x(g + 2)
                        pe.wait_ge(S("e_actT"), g + 1)
                        for k in range(KT):
                            if k % 4 == 0:
                                landed(4 + k // 4)
                            w = ring[:, slots[4 + k // 4], :].rearrange("p (k n) -> p k n", k=4)
                            for h in range(2):
                                last = mm(B(3)[CAP * h:CAP * (h + 1), :], act[:, k % 4, k // 4, :],
                                          w[:, k % 4, 512 * h:512 * (h + 1)], start=k == 0, stop=k == KT - 1)
                        last.then_inc(S("e_down"), 1)
            g = pe.snap(pg)
            pe.wait_ge(S("e_ye"), g + 1)
            pe.wait_ge(S("e_selT"), g + 1)
            scatter().then_inc(S("moe_done"), 1)

            def arrived2(n):
                pe.wait_ge(S(f"post_in{n % PRO_RING}"), 16 * (n // PRO_RING + 1))

            pe.wait_ge(S("mem_in"), 16)
            for b in range(4):
                for k in (2 * b, 2 * b + 1):
                    for i in range(TT):
                        last = tr(bank2(b)[:, k % 2, i * P:(i + 1) * P], tok[:, i, k * P:(k + 1) * P])
                last.then_inc(S("mem_turned"), 1)
            pe.wait_ge(S("memT_ready"), 4)
            pe.wait_ge(*at("x3_ready"))
            job = 0

            def lin_bank():
                if job >= 4:
                    pe.wait_ge(S("lin_copied"), job - 3)
                return job % 4

            for n in range(6):
                arrived2(n)
                w = slot8(n % PRO_RING)
                for half in range(2):
                    b = lin_bank()
                    if n == 3:
                        for k in range(KT):
                            last = mm(B(b), xT[:, k, half * P:(half + 1) * P], w[:, k, :],
                                      start=k == 0, stop=k == KT - 1)
                    elif (n == 4 and half == 0) or (n == 5 and half == 1):
                        src = xT if n == 4 else memT
                        for i in range(TT):
                            for k in range(KT):
                                last = mm(bank2(b)[:, i, :], src[:, k, i * P:(i + 1) * P],
                                          w[:, k, half * T:(half + 1) * T], start=k == 0, stop=k == KT - 1)
                    else:
                        src = memT if n == 5 else xT
                        for jj in range(2):
                            for k in range(KT):
                                c0 = (2 * half + jj) * P
                                last = mm(bank2(b)[:, jj, :], w[:, k, c0:c0 + P], src[:, k, :],
                                          start=k == 0, stop=k == KT - 1)
                    last.then_inc(S("halves_used"), 1)
                    job += 1
            pe.wait_ge(S("lin_copied"), 12)

            def sb_scores(i):
                for par_ in range(2):
                    b, p0 = [(4, 5), (0, 1)][i % 2][par_], HD * par_
                    q, k = sbq[p0:p0 + HD, i, :], sbq[p0:p0 + HD, 6 + i, :]
                    mm(B(b)[:, 0:T], k[:, 0:P], q, start=True, stop=True)
                    last = mm(B(b)[:, T:3 * P], k[:, P:T], q[:, P:T], start=True, stop=True)
                last.then_inc(S("sb_s"), 1)

            sb_scores(0)
            for i in range(6):
                if i + 1 < 6:
                    sb_scores(i + 1)
                pe.wait_ge(S("sb_sp"), i + 1)
                for par_ in range(2):
                    mm(B(6 + par_)[:, 0:T], rev_tri[:, :], sp[:, par_, 0:T], start=True, stop=False,
                       skip_group_check=True)
                    mm(B(6 + par_)[:, P:T], ones[:, :], sp[:, par_, T:3 * P], start=False, stop=False,
                       skip_group_check=True)
                    last = mm(B(6 + par_)[:, T:3 * P], rev_tri[:, :], sp[:, par_, T:3 * P], start=False, stop=True,
                              skip_group_check=True)
                last.then_inc(S("sb_acc"), 1)
                pe.wait_ge(S("sb_w"), i + 1)
                for par_ in range(2):
                    h, p0 = 2 * i + par_, HD * par_
                    o = B(2 + i % 2)
                    mm(o[p0:p0 + HD, 0:T], sbv[:, 0, h * HD:(h + 1) * HD], dd[:, par_, 0:T],
                       start=True, stop=False, skip_group_check=True)
                    last = mm(o[p0:p0 + HD, P:T], sbv[:, 1, h * HD:(h + 1) * HD], dd[:, par_, T:3 * P],
                              start=False, stop=True, skip_group_check=True)
                last.then_inc(S("sb_o"), 1)
            for i in range(2):
                if i:
                    pe.wait_ge(S("mem_p"), i)
                else:
                    pe.wait_ge(S("sb_oc"), 6)
                for par_ in range(2):
                    p0 = HD * par_
                    for ti in range(TT):
                        last = mm(B(4 + par_)[:, ti * T:(ti + 1) * T], qm[p0:p0 + HD, i, ti * P:(ti + 1) * P],
                                  km[p0:p0 + HD, i, :], start=True, stop=True)
                last.then_inc(S("mem_s"), 1)
                pe.wait_ge(S("mem_p"), i + 1)
                for par_ in range(2):
                    for mi in range(2):
                        for ti in range(TT):
                            last = tr(B(6 + par_)[:, (mi * 2 + ti) * P:(mi * 2 + ti + 1) * P],
                                      ms[:, par_, ti, mi * P:(mi + 1) * P])
                last.then_inc(S("mem_t"), 1)
                pe.wait_ge(S("mem_tc"), i + 1)
                for par_ in range(2):
                    h, p0 = 2 * i + par_, HD * par_
                    for mi in range(2):
                        last = mm(B(2 + i)[p0:p0 + HD, 0:T], vmem[:, mi, h * HD:(h + 1) * HD], mpt[:, par_, mi, :],
                                  start=mi == 0, stop=mi == 1)
                last.then_inc(S("mem_o"), 1)
            pe.wait_ge(S("mem_oc"), 2)
            for n in (6, 7):
                arrived2(n)
                w = slot8(n % PRO_RING)
                for half in range(2):
                    b = 4 + 2 * (n - 6) + half
                    for jj in range(2):
                        for k in range(KT):
                            c0 = (2 * half + jj) * P
                            last = mm(bank2(b)[:, jj, :], w[:, k, c0:c0 + P], yT[:, k, :],
                                      start=k == 0, stop=k == KT - 1)
                    last.then_inc(S("halves_used"), 1)

            def ln_sums(r, src_mean, src_var):
                pe.wait_ge(S("ln_z"), r + 1)
                for k in range(KT):
                    last = mm(B(0)[:, 0:T], ones[:, :], src_mean[:, k, :], start=k == 0, stop=k == KT - 1)
                last.then_inc(S("ln_mean"), 1)
                pe.wait_ge(S("ln_sq"), r + 1)
                for k in range(KT):
                    last = mm(B(1)[:, 0:T], ones[:, :], src_var[:, k, :], start=k == 0, stop=k == KT - 1)
                last.then_inc(S("ln_var"), 1)

            ln_sums(0, xT, hT)
            pe.wait_ge(S("ln_done"), 1)
            job = 0
            for n in range(8, 16):
                arrived2(n)
                w = slot8(n % PRO_RING)
                for half in range(2):
                    if job >= 4:
                        pe.wait_ge(S("up_read"), job - 3)
                    b = job % 4
                    for jj in range(2):
                        for k in range(KT):
                            c0 = (2 * half + jj) * P
                            last = mm(bank2(b)[:, jj, :], w[:, k, c0:c0 + P], xT[:, k, :],
                                      start=k == 0, stop=k == KT - 1)
                    last.then_inc(S("halves_used"), 1)
                    job += 1
            for n in range(16, 24):
                arrived2(n)
                w = ring[:, n % PRO_RING, :].rearrange("p (k n) -> p k n", k=4)
                for kk_ in range(4):
                    k = 4 * (n - 16) + kk_
                    pe.wait_ge(S("up_read"), k // 2 + 1)
                    for m in range(KT):
                        last = mm(bank2(4 + m // 2)[:, m % 2, :], w[:, kk_, m * P:(m + 1) * P], hid[:, k, :],
                                  start=k == 0 and m % 2 == 0, stop=k == 31, skip_group_check=True)
                    if kk_ % 2:
                        last.then_inc(S("halves_used"), 1)
            ln_sums(1, xT, hT)
            pe.wait_ge(S("ln_done"), 2)
            for b in range(4):
                for jj in range(2):
                    for i in range(TT):
                        k = 2 * b + jj
                        last = tr(B(4 + b)[:, (i * 2 + jj) * P:(i * 2 + jj + 1) * P], xT[:, k, i * P:(i + 1) * P])
                last.then_inc(S("out_turned"), 1)

        @block.scalar
        def _(ac):
            ch = Chain(ac, S("act_chain"))
            A = nc.scalar.activation

            def dma(dst, src, sem):
                nc.scalar.dma_start(dst, src).then_inc(sem, 16)

            def rows(name):
                v = a[name]
                v = v[0] if len(v.shape) == 2 else v[0].rearrange("a b -> (a b)")
                return v.rearrange("(r c) -> r c", c=P)

            dma(tok[:, :, :], a["x"][0].rearrange("(i p) d -> p i d", p=P), S("x_in"))
            ac.wait_ge(S("prow_zero"), 1)
            n_dma = 0
            for name, key in [("b_ada", "b_ada"), ("c", "c"), ("norm1_g", "norm1_g"), ("norm2_g", "norm2_g"),
                              ("w0", "rwkv_w0"), ("a0", "rwkv_a0"), ("k_k", "rwkv_k_k"), ("k_a", "rwkv_k_a"),
                              ("r_k", "rwkv_r_k"), ("ln_g", "rwkv_ln_g"), ("ln_b", "rwkv_ln_b")]:
                src = rows(key)
                dma(prow[ROW[name]:ROW[name] + src.shape[0], :], src, S("par_in"))
                n_dma += 1
            mu = a["rwkv_mu"]
            dma(prow[ROW["mu"]:ROW["mu"] + 14, :], mu[0, 0:14 * P].rearrange("(r c) -> r c", c=P), S("par_in"))
            dma(prow[ROW["mu"] + 14:ROW["mu"] + 15, 0:32], mu[:, 14 * P:14 * P + 32], S("par_in"))
            n_dma += 2
            for name, key in [("qn", "q_norm_g"), ("kn", "k_norm_g")]:
                for c0 in (0, HD):
                    dma(prow[ROW[name]:ROW[name] + 1, c0:c0 + HD], a[key], S("par_in"))
                    n_dma += 1
            for j, key in enumerate(["ln_mix_g_2", "ln_mix_b_2", "ln_ffn_g_2", "ln_ffn_b_2"]):
                dma(prow2[8 * j:8 * j + 8, :], rows(key), S("par_in"))
                n_dma += 1
            assert n_dma == N_PAR_DMA
            dma(wl[0:LOW, 0, :], a["rwkv_w_up"][0], S("wl_in"))
            dma(wl[LOW:P, 0, :], a["rwkv_a_up"][0], S("wl_in"))
            dma(wl[:, 1, :], a["rwkv_g_up"][0, 0:P, :], S("wl_in"))
            dma(wl[0:GLOW - P, 2, :], a["rwkv_g_up"][0, P:GLOW, :], S("wl_in"))
            dma(w_rout[:, :, :], a["w_router"][0].rearrange("(k p) n -> p k n", p=P), S("rout_in"))
            dma(b_rout[:, :], a["b_router"], S("rout_in"))

            for n, b in enumerate((4, 6)):
                ac.wait_ge(S("x_turned"), b - 3)
                A(xT[:, 2 * (b - 4):2 * (b - 4) + 2, :], bank2(b), ACT.Copy).then_inc(S("xcopy_a"), 1)
                A(hT[:, 2 * (b - 4):2 * (b - 4) + 2, :], bank2(b), ACT.Square).then_inc(S("xsq_a"), 1)
            ac.wait_ge(*at("par_turned"))
            ch.link(A(par[:, :], B(1)[:, 0:N_ROWS + N_ROWS2], ACT.Copy))
            A(sigc[:, :], par[:, ROW["c"]:ROW["c"] + KT], ACT.Sigmoid).then_inc(*mark("sigc_ready"))
            ac.wait_ge(*at("xss"))
            ac.wait_ge(*at("eps_ready"))
            A(rstd[:, :], B(3)[:, 0:T], ACT.Sqrt, bias=small[:, 0:1], scale=1.0 / D).then_inc(S("rs_ready"), 1)
            for n in range(12):
                ac.wait_ge(S("halves_used"), 2 * n + 2)
                if n >= 2:
                    ac.wait_ge(S("ada_turned"), n - 1)
                A(ada_sb[n % 2], B([0, 4][n % 2]), ACT.Copy).then_inc(S("ada_copied"), 1)
            ac.wait_ge(S("xn_ready"), 1)
            ac.wait_ge(*at("mods_ready"))
            for k in range(KT):
                last = A(hT[:, k, :], hT[:, k, :], ACT.Identity, bias=mods[:, k:k + 1], scale=sc1[:, k:k + 1])
            last.then_inc(*mark("h_ready"))

            job = 0

            def proj_copies(dsts):
                nonlocal job
                for dst in dsts:
                    ac.wait_ge(S("halves_used"), 24 + job + 1)
                    b = 1 + job % 4
                    if dst.shape[0] < P:
                        last = A(dst, B(b)[0:dst.shape[0], 0:T], ACT.Copy)
                    elif len(dst.shape) == 3:
                        last = A(dst, bank2(b), ACT.Copy)
                    else:
                        last = A(dst, B(b), ACT.Copy)
                    last.then_inc(S("proj_copied"), 1)
                    job += 1

            proj_copies([praw[0][:, 0:2, 1:T + 1], praw[0][0:GLOW - P, 2, 1:T + 1]])
            proj_copies([praw[1][:, 0:2, 1:T + 1], praw[1][:, 2:4, 1:T + 1]])
            ac.wait_ge(S("mixed"), 1)
            A(lo[0:LOW, 0, :], lo[0:LOW, 0, :], ACT.Tanh).then_inc(*mark("tanh_ready"))
            A(lo[:, 1, :], lo[:, 1, :], ACT.Sigmoid)
            A(lo[0:GLOW - P, 2, :], lo[0:GLOW - P, 2, :], ACT.Sigmoid).then_inc(*mark("gate_sig"))
            proj_copies([praw[0][:, 0:2, 1:T + 1], praw[0][:, 2:4, 1:T + 1]])
            ac.wait_ge(*at("lora_w"))
            for m in range(RT):
                last = A(sg[:, m, :], bank2(5 + m // 2)[:, m % 2, :], ACT.Sigmoid,
                         bias=par[:, ROW["w0"] + m:ROW["w0"] + m + 1])
            last.then_inc(*mark("sg_ready"))
            ac.wait_ge(*at("lora_a"))
            for m in range(RT):
                last = A(aT[:, m, :], bank2([7, 0][m // 2])[:, m % 2, :], ACT.Sigmoid,
                         bias=par[:, ROW["a0"] + m:ROW["a0"] + m + 1])
            last.then_inc(*mark("a_ready"))
            ac.wait_ge(S("mixed"), 2)
            proj_copies([praw[1][:, 0:2, 1:T + 1], praw[1][:, 2:4, 1:T + 1]])
            kif = ki.rearrange("p m c t -> p m (c t)")
            ac.wait_ge(*at("kk_raw"))
            A(kif, kk, ACT.Square).then_inc(*mark("kksq"))
            ac.wait_ge(*at("lora_g"))
            for j in range(2):
                last = A(gT[:, 2 * j:2 * j + 2, :], bank2(5 + j), ACT.Copy)
            last.then_inc(*mark("g_copied"))
            ac.wait_ge(*at("kkss"))
            for j in range(2):
                last = A(kif[:, 2 * j:2 * j + 2, :], bank2([7, 0][j]), ACT.Sqrt)
            last.then_inc(*mark("kk_norm"))
            proj_copies([qk[:, 0:2, :], qk[:, 2:4, :], qk[:, 4:6, :], qk[:, 6:8, :]])
            ch.link(nc.scalar.copy(small[:, 8:9], small[:, 0:1]))
            A(tok_f, view(work_f, 2056, [2048]), ACT.Square).then_inc(*mark("qksq"))
            proj_copies([vm[:, 0, :], vm[:, 1, :]])
            ac.wait_ge(*at("q_ready"))
            ac.wait_ge(*at("kk_ready"))
            q4 = q_cum.rearrange("p m (c t) -> p m c t", c=TT)
            dq4 = sg.rearrange("p m (c t) -> p m c t", c=TT)
            A(kr[:, :, :, 1, :], q4, ACT.Exp, scale=-EXP_HALF)
            A(kr[:, :, :, 0, :], dq4, ACT.Exp, scale=-EXP_HALF)
            A(ki, q4, ACT.Exp, scale=EXP_HALF).then_inc(*mark("decays"))
            ac.wait_ge(*at("fac_arg"))
            A(fac[:, :], fac[:, :], ACT.Exp, scale=-EXP_HALF).then_inc(*mark("fac_ready"))
            ac.wait_ge(*at("vturned"))
            A(vtok[:, 0, :], B(5), ACT.Copy)
            A(vtok[:, 1, :], B(6), ACT.Copy).then_inc(*mark("vtok_ready"))
            ac.wait_ge(*at("qkss"))
            for j in range(4):
                last = A(yT[:, 2 * j:2 * j + 2, :], bank2(1 + j), ACT.Sqrt, bias=small[:, 0:1], scale=1.0 / HD)
            last.then_inc(*mark("qk_rs"))
            ac.wait_ge(*at("biki_turned"))
            A(bitok, B(5), ACT.Copy, scale=-1.0)
            A(kitok, B(6), ACT.Copy).then_inc(*mark("biki_tok"))
            for i in range(RT):
                ac.wait_ge(S("moba_m"), i + 1)
                for par_ in range(2):
                    for ti in range(TT):
                        v = sc_p[:, par_, 0:P] if ti == 0 else sc_p[:, par_, P:3 * P]
                        c0 = 16 + ti * 2 + par_
                        last = A(v, v, ACT.Exp, bias=small[:, c0:c0 + 1], scale=ATT_SCALE,
                                 accum_out=small[:, c0 + 4:c0 + 5])
                last.then_inc(S("moba_e"), 1)
                ac.wait_ge(S("moba_t"), i + 1)
                A(pt_p[:, 0, :], B(3)[:, 0:3 * P], ACT.Copy)
                A(pt_p[:, 1, :], B(4)[:, 0:3 * P], ACT.Copy).then_inc(S("moba_tc"), 1)
                ac.wait_ge(S("moba_o"), i + 1)
                A(yT[:, 4 + i, :], B(5 + i % 2)[:, 0:T], ACT.Copy).then_inc(S("moba_oc"), 1)
            for gi in range(4):
                c, hh = gi // 2, gi % 2
                for l in range(1, 6):
                    ac.wait_ge(S("bt_used"), 6 * gi + l)
                    A(y_inv, B(6).rearrange("p (q t) -> p q t", q=4), ACT.Copy).then_inc(S("y_copied"), 1)
                ac.wait_ge(S("r_done"), gi + 1)
                A(rr[:, 0:2, :], B(5)[:, 0:P].rearrange("p (q t) -> p q t", q=2), ACT.Copy)
                A(rr[:, 2:4, :], B(6)[:, 0:P].rearrange("p (q t) -> p q t", q=2), ACT.Copy).then_inc(S("r_copied"), 1)
                ac.wait_ge(S("w_done"), 2 * gi + 1)
                A(w1, B(7)[:, 0:T].rearrange("p (q t) -> p q t", q=4), ACT.Copy).then_inc(S("w_copied"), 1)
                ac.wait_ge(S("bt_used"), 6 * gi + 6)
                A(w2, B(4)[:, 0:T].rearrange("p (q t) -> p q t", q=4), ACT.Copy).then_inc(S("w_copied"), 1)
                ac.wait_ge(S("yo_done"), gi + 1)
                A(yT[:, 2 * hh:2 * hh + 2, c * P:(c + 1) * P], B(5)[:, 0:T].rearrange("p (q t) -> p q t", q=2),
                  ACT.Copy).then_inc(S("yo_copied"), 1)
            gsq = view(tok_f, 0, [RT, T])
            gmean = view(tok_f, 1024, [RT, T])
            ac.wait_ge(*at("gn_mean"))
            for j in range(2):
                last = A(gmean[:, 2 * j:2 * j + 2, :], bank2(j), ACT.Copy, scale=1.0 / HD)
            last.then_inc(*mark("gn_meanc"))
            ac.wait_ge(*at("gn_cent"))
            A(gsq, yT[:, 0:RT, :], ACT.Square).then_inc(*mark("gn_sq"))
            ac.wait_ge(*at("gn_var"))
            for j in range(2):
                last = A(gmean[:, 2 * j:2 * j + 2, :], bank2(2 + j), ACT.Sqrt, bias=small[:, 1:2], scale=1.0 / HD)
            last.then_inc(*mark("gn_rs"))
            ac.wait_ge(*at("x2_ready"))
            dma(b_down, a["b_down"][0], S("b_down_in"))
            A(hT[:, :, :], xT[:, :, :], ACT.Square).then_inc(*mark("x2sq"))
            ac.wait_ge(*at("x2ss"))
            A(rstd[:, :], B(0)[:, 0:T], ACT.Sqrt, bias=small[:, 0:1], scale=1.0 / D).then_inc(S("rs_ready"), 1)
            ac.wait_ge(S("xn_ready"), 2)
            for k in range(KT):
                last = A(hT[:, k, :], hT[:, k, :], ACT.Identity, bias=mods[:, 24 + k:25 + k], scale=sc2[:, k:k + 1])
            last.then_inc(*mark("h2_ready"))
            ac.wait_ge(S("h2_turned"), 4)
            dma(bgu, a["b_gate_up"][0], S("bgu_in"))
            for b in (0, 2):
                ac.wait_ge(S("h2_turned"), b + 1)
                A(tok[:, :, 2 * b * P:(2 * b + 2) * P], B(4 + b).rearrange("p (i x) -> p i x", i=2),
                  ACT.Copy).then_inc(S("h2tok_a"), 1)
            ac.wait_ge(*at("sel_mask"))
            for i in range(TT):
                last = A(prob[:, i, :], logit[:, i, :], ACT.Exp, bias=small[:, 40 + i:41 + i])
            last.then_inc(*mark("prob_e"))

            def x_out(g):
                ac.wait_ge(S("e_gather"), g)
                A(x_tm, B(0), ACT.Copy).then_inc(S("e_xtm"), 1)

            def xe_out(g):
                ac.wait_ge(S("e_xturn"), g)
                A(xe.rearrange("p c h s -> p (c h s)"), B(0), ACT.Copy).then_inc(S("e_xe"), 1)

            ac.wait_ge(*at("zeroed"))
            ac.sem_inc(S("e_ye"), 1)
            x_out(1)
            xe_out(1)
            ac.wait_ge(*at("npass_ready"))
            total = ac.value_load(cum[0:1, E_N - 1:E_N], min_val=E_N, max_val=N_ITEM - 1)
            with ac.Fori(0, total) as g:
                ac.wait_ge(S("e_gate"), g + 1)
                A(sgm, gt, ACT.Sigmoid, scale=1.702).then_inc(S("e_sig"), 1)
                x_out(g + 2)
                ac.wait_ge(S("e_actturn"), g + 1)
                A(act.rearrange("p c h s -> p (c h s)"), B(3), ACT.Copy).then_inc(S("e_actT"), 1)
                xe_out(g + 2)
                ac.wait_ge(S("e_down"), g + 1)
                A(ye, B(3), ACT.Copy).then_inc(S("e_ye"), 1)

            dma(tok[:, :, :], a["mem_2"][0].rearrange("(i p) d -> p i d", p=P), S("mem_in"))
            for b in range(4):
                ac.wait_ge(S("mem_turned"), b + 1)
                A(memT[:, 2 * b:2 * b + 2, :], bank2(b), ACT.Copy).then_inc(S("memT_ready"), 1)
            dsts = [sbq[:, 2 * j:2 * j + 2, :] for j in range(6)]
            dsts += [sbv[:, i, 0:512] for i in range(TT)] + [sbv[:, :, 512:SB_W], qm, km, vmem]
            for job, dst in enumerate(dsts):
                ac.wait_ge(S("halves_used"), 2 * N_PRO + job + 1)
                src = B(job % 4) if len(dst.shape) == 2 else bank2(job % 4)
                A(dst, src, ACT.Copy).then_inc(S("lin_copied"), 1)

            def pairv(b0, b1, i):
                return [B(b0)[:, 0:3 * P], B(b1)[:, 0:3 * P]][i]

            for i in range(6):
                b = [(4, 5), (0, 1)][i % 2]
                ac.wait_ge(S("sb_s"), i + 1)
                if i:
                    ac.wait_ge(S("sb_d"), i)
                for par_ in range(2):
                    ch.add(A(zs[:, par_, :], B(b[par_])[:, 0:3 * P], ACT.Copy, scale=ATT_SCALE))
                ch.wait()
                ch.link(A(ee, zs, ACT.Abs))
                ch.link(A(ee, ee, ACT.Exp, scale=-1.0))
                A(ee, ee, ACT.Ln, bias=1.0).then_inc(S("sb_ln"), 1)
                ac.wait_ge(S("sb_d"), i + 1)
                A(dd, dd, ACT.Exp).then_inc(S("sb_w"), 1)
                ac.wait_ge(S("sb_o"), i + 1)
                A(yT[:, i, :], B(2 + i % 2)[:, 0:T], ACT.Copy).then_inc(S("sb_oc"), 1)
            for i in range(2):
                ac.wait_ge(S("mem_m"), i + 1)
                for par_ in range(2):
                    for ti in range(TT):
                        c0 = 16 + ti + 2 * par_
                        last = A(ms[:, par_, ti, :], B(4 + par_)[:, ti * T:(ti + 1) * T], ACT.Exp,
                                 bias=small[:, c0:c0 + 1], scale=ATT_SCALE, accum_out=small[:, c0 + 4:c0 + 5])
                last.then_inc(S("mem_e"), 1)
                ac.wait_ge(S("mem_t"), i + 1)
                for par_ in range(2):
                    last = A(mpt[:, par_, :, :], bank2(6 + par_), ACT.Copy)
                last.then_inc(S("mem_tc"), 1)
                ac.wait_ge(S("mem_o"), i + 1)
                A(yT[:, 6 + i, :], B(2 + i)[:, 0:T], ACT.Copy).then_inc(S("mem_oc"), 1)

            def ln(r):
                ac.wait_ge(S("ln_mean"), r + 1)
                A(rstd[:, :], B(0)[:, 0:T], ACT.Copy, scale=1.0 / D).then_inc(S("ln_meanc"), 1)
                ac.wait_ge(S("ln_cent"), r + 1)
                A(hT[:, :, :], xT[:, :, :], ACT.Square).then_inc(S("ln_sq"), 1)
                ac.wait_ge(S("ln_var"), r + 1)
                A(rstd[:, :], B(1)[:, 0:T], ACT.Sqrt, bias=small[:, 2:3], scale=1.0 / D).then_inc(S("ln_rs"), 1)
                ac.wait_ge(S("ln_scaled"), r + 1)
                g0, b0 = (ROW2["lnm_g"], ROW2["lnm_b"]) if r == 0 else (ROW2["lnf_g"], ROW2["lnf_b"])
                for k in range(KT):
                    last = A(xT[:, k, :], xT[:, k, :], ACT.Identity, bias=par[:, b0 + k:b0 + k + 1],
                             scale=par[:, g0 + k:g0 + k + 1])
                last.then_inc(S("ln_done"), 1)

            ln(0)
            for job in range(16):
                ac.wait_ge(S("halves_used"), 2 * (N_PRO + 8) + job + 1)
                if job >= 2:
                    ac.wait_ge(S("up_read"), job - 1)
                A(fr[:, job % 2, :, :], bank2(job % 4), ACT.Relu).then_inc(S("up_relu"), 1)
            ln(1)
            for b in (0, 2):
                ac.wait_ge(S("out_turned"), b + 1)
                A(tok[:, :, 2 * b * P:(2 * b + 2) * P], B(4 + b).rearrange("p (i x) -> p i x", i=2),
                  ACT.Copy).then_inc(S("out_ready_a"), 1)

        @block.vector
        def _(ve):
            ch = Chain(ve, S("dve_chain"))
            V = nc.vector

            def col(name, m, n=1):
                r = (ROW if name in ROW else ROW2)[name]
                return par[:, r + m:r + m + n]

            ch.add(V.memset(small[:, 0:1], 1e-6))
            ch.add(V.memset(small[:, 1:2], 64e-5))
            ch.add(V.memset(small[:, 2:3], 1e-5))
            V.memset(small[:, 3:64], 0.0).then_inc(*mark("eps_ready"))
            for n, b in enumerate((5, 7)):
                ve.wait_ge(S("x_turned"), b - 3)
                V.tensor_copy(xT[:, 2 * (b - 4):2 * (b - 4) + 2, :], bank2(b)).then_inc(S("xcopy_d"), 1)
            ve.wait_ge(S("xcopy_d"), 2)
            V.tensor_tensor(hT[:, 2:4, :], xT[:, 2:4, :], xT[:, 2:4, :], ALU.mult)
            V.tensor_tensor(hT[:, 6:8, :], xT[:, 6:8, :], xT[:, 6:8, :], ALU.mult).then_inc(*mark("xsq_d"))
            ve.wait_ge(*at("sigc_ready"))
            V.tensor_tensor(silc, col("c", 0, KT).unsqueeze(2).broadcast_to([P, KT, 32]),
                            sigc[:, :].unsqueeze(2).broadcast_to([P, KT, 32]), ALU.mult)\
                .then_inc(*mark("silc_ready"))
            ve.wait_ge(S("rs_ready"), 1)
            ch.link(V.reciprocal(rstd[:, :], rstd[:, :]))
            ve.wait_ge(S("xcopy_a"), 2)
            rb = rstd[:, :].unsqueeze(1).broadcast_to([P, KT, T])
            V.tensor_tensor(hT[:, :, :], xT[:, :, :], rb, ALU.mult).then_inc(S("xn_ready"), 1)
            for n in range(12):
                ve.wait_ge(S("ada_turned"), n + 1)
                turned = B(5 + n % 2).rearrange("p (j q r) -> p j q r", j=4, q=4)
                V.tensor_reduce(mods[:, 4 * n:4 * n + 4], turned[:, :, :, 0], AX.X, ALU.add).then_inc(S("ada_summed"), 1)
            ve.wait_ge(S("ada_summed"), 12)
            ch.link(V.tensor_tensor(mods[:, :], mods[:, :], par[:, 0:48], ALU.add))
            ch.add(V.scalar_tensor_tensor(out=sc1[:, :], in0=mods[:, 8:16], scalar=1.0, in1=col("norm1_g", 0, 8),
                                          op0=ALU.add, op1=ALU.mult))
            V.scalar_tensor_tensor(out=sc2[:, :], in0=mods[:, 32:40], scalar=1.0, in1=col("norm2_g", 0, 8),
                                   op0=ALU.add, op1=ALU.mult).then_inc(*mark("mods_ready"))

            def mix_chunk(pr, dst, mu0, widths, copied):
                ve.wait_ge(S("proj_copied"), copied)
                if copied > 2:
                    ve.wait_ge(S("mixed"), copied // 2 - 1)
                n = len(widths)
                full = sum(w == P for w in widths)
                ch.add(V.tensor_tensor(k2[:, 0:full, :], pr[:, 0:full, 0:T], pr[:, 0:full, 1:T + 1], ALU.subtract))
                if full < n:
                    w = widths[-1]
                    ch.add(V.tensor_tensor(k2[0:w, full, :], pr[0:w, full, 0:T], pr[0:w, full, 1:T + 1],
                                           ALU.subtract))
                ch.wait()
                for j, w in enumerate(widths):
                    last = V.scalar_tensor_tensor(out=dst[0:w, j, :], in0=k2[0:w, j, :],
                                                  scalar=par[0:w, ROW["mu"] + mu0 + j:ROW["mu"] + mu0 + j + 1],
                                                  in1=pr[0:w, j, 1:T + 1], op0=ALU.mult, op1=ALU.add)
                last.then_inc(S("mixed"), 1)

            ve.wait_ge(*at("mods_ready"))
            mix_chunk(praw[0], lo, 12, [P, P, GLOW - P], 2)
            mix_chunk(praw[1], k_m, 4, [P] * 4, 4)
            ve.wait_ge(S("mixed"), 2)
            V.tensor_tensor(kk, k_m, col("k_k", 0, 4).unsqueeze(2).broadcast_to([P, RT, T]), ALU.mult)\
                .then_inc(*mark("kk_raw"))
            mix_chunk(praw[0], r_m, 0, [P] * 4, 6)
            ve.wait_ge(*at("sg_ready"))
            ve.wait_ge(S("consts"), 1)
            for m in range(RT):
                for c in range(TT):
                    t0 = c * P
                    ch.add(V.tensor_tensor_scan(q_cum[:, m, t0:t0 + P], ones[:, :], sg[:, m, t0:t0 + P], 0.0,
                                                ALU.mult, ALU.add))
            ch.wait()
            qf = q_cum.rearrange("p m (c t) -> p (m c) t", c=TT)
            ch.link(V.tensor_copy(qmid[:, :], qf[:, :, 63]))
            ch.link(V.tensor_tensor(qf, qf, qmid[:, :].unsqueeze(2).broadcast_to([P, RT * TT, P]), ALU.subtract))
            V.tensor_tensor(sg, q_cum, sg, ALU.subtract).then_inc(*mark("q_ready"))
            V.tensor_tensor(fac[:, :], qf[:, 0:8:2, P - 1], qmid[:, 1:8:2], ALU.add).then_inc(*mark("fac_arg"))
            mix_chunk(praw[1], v_m, 8, [P] * 4, 8)
            kif = ki.rearrange("p m c t -> p m (c t)")
            ve.wait_ge(*at("kk_norm"))
            ch.link(V.tensor_scalar(kif, kif, 1e-12, None, ALU.max))
            ch.link(V.reciprocal(kif, kif))
            V.tensor_tensor(kk, kk, kif, ALU.mult).then_inc(*mark("kk_ready"))
            ve.wait_ge(*at("a_ready"))
            ve.wait_ge(S("mixed"), 4)
            for m in range(RT):
                ch.add(V.tensor_scalar(k2[:, m, :], aT[:, m, :], 1.0, col("k_a", m), ALU.subtract, ALU.mult))
            ch.wait()
            ch.link(V.scalar_tensor_tensor(out=k2, in0=k2, scalar=1.0, in1=k_m, op0=ALU.add, op1=ALU.mult))
            ch.link(V.tensor_tensor(bonus, r_m, k2, ALU.mult))
            for m in range(RT):
                last = V.tensor_scalar(bonus[:, m, :], bonus[:, m, :], col("r_k", m), None, ALU.mult)
            last.then_inc(*mark("rk_ready"))

            def c4(v):
                return v.rearrange("p m (c t) -> p m c t", c=TT)

            ve.wait_ge(*at("kk_ready"))
            ch.link(V.tensor_tensor(bi, c4(kk), c4(aT), ALU.mult))
            ve.wait_ge(*at("decays"))
            ch.link(V.tensor_tensor(bi, bi, ki, ALU.mult))
            V.tensor_tensor(ki, ki, c4(k2), ALU.mult).then_inc(*mark("biki_ready"))
            V.tensor_tensor(kr[:, :, :, 0, :], kr[:, :, :, 0, :], c4(kk), ALU.mult)
            V.tensor_tensor(kr[:, :, :, 1, :], kr[:, :, :, 1, :], c4(r_m), ALU.mult).then_inc(S("kr_ready"), 1)
            ve.wait_ge(*at("qk_rs"))
            ch.link(V.reciprocal(yT[:, :, :], yT[:, :, :]))
            ch.link(V.tensor_tensor(qk, qk, yT[:, :, :], ALU.mult))
            ch.add(V.tensor_scalar(qk[:, 0:4, :], qk[:, 0:4, :], col("qn", 0), None, ALU.mult))
            V.tensor_scalar(qk[:, 4:8, :], qk[:, 4:8, :], col("kn", 0), None, ALU.mult).then_inc(*mark("qk_ready"))
            ve.wait_ge(*at("bonss"))
            for j in range(2):
                last = V.tensor_tensor(bonus[:, 2 * j:2 * j + 2, :], bank2([7, 0][j]), v_m[:, 2 * j:2 * j + 2, :],
                                       ALU.mult)
            last.then_inc(*mark("bonus_ready"))
            for i in range(RT):
                b = [(1, 2), (7, 0)][i % 2]
                ve.wait_ge(S("moba_s"), i + 1)
                if i:
                    ve.wait_ge(S("moba_t"), i)
                for par_ in range(2):
                    slope = 2.0 ** (-(2 * i + par_ + 1))
                    ch.add(V.scalar_tensor_tensor(out=sc_p[:, par_, :], in0=alibi[:, :], scalar=slope / ATT_SCALE,
                                                  in1=B(b[par_])[:, 0:3 * P], op0=ALU.mult, op1=ALU.add))
                ch.wait()
                ch.add(V.tensor_reduce(small[:, 24:26], sc_p[:, :, 0:P], AX.X, ALU.max))
                ch.add(V.tensor_reduce(small[:, 26:28], sc_p[:, :, P:3 * P], AX.X, ALU.max))
                ch.wait()
                V.tensor_scalar(small[:, 16:20], small[:, 24:28], -ATT_SCALE, None, ALU.mult).then_inc(S("moba_m"), 1)
                ve.wait_ge(S("moba_e"), i + 1)
                ch.link(V.reciprocal(small[:, 28:32], small[:, 20:24]))
                V.tensor_tensor(sc_p[:, :, 0:P], sc_p[:, :, 0:P],
                                small[:, 28:30].unsqueeze(2).broadcast_to([P, 2, P]), ALU.mult)
                V.tensor_tensor(sc_p[:, :, P:3 * P], sc_p[:, :, P:3 * P],
                                small[:, 30:32].unsqueeze(2).broadcast_to([P, 2, T]), ALU.mult)\
                    .then_inc(S("moba_p"), 1)

            def b4(v):
                return v.unsqueeze(1).broadcast_to([P, 4, P])

            ve.wait_ge(S("moba_t"), RT)
            for gi in range(4):
                c, hh = gi // 2, gi % 2
                ve.wait_ge(S("grp_m"), 3 * gi + 1)
                for j in range(2):
                    last = V.tensor_tensor(atr[:, 2 * j:2 * j + 2, :], bank2(j),
                                           mask_b[:, :].unsqueeze(1).broadcast_to([P, 2, T]), ALU.mult)
                last.then_inc(S("atr_ready"), 1)
                ve.wait_ge(S("grp_m"), 3 * gi + 2)
                for j in range(2):
                    ch.add(V.tensor_tensor(x_inv[:, 2 * j:2 * j + 2, :],
                                           B(4 + j)[:, 0:T].rearrange("p (q t) -> p q t", q=2),
                                           lvl0n[:, :].unsqueeze(1).broadcast_to([P, 2, P]), ALU.mult))
                ve.wait_ge(S("atr_ready"), gi + 1)
                ch.add(V.tensor_tensor(xt_inv, atr[:, :, 0:P], b4(lvl[:, 0, :]), ALU.mult))
                ch.wait()
                V.tensor_tensor(x_inv, x_inv, b4(ident[:, :]), ALU.add).then_inc(S("x_ready"), 1)
                V.tensor_tensor(xt_inv, xt_inv, b4(ident[:, :]), ALU.add).then_inc(S("xt_ready"), 1)
                ve.wait_ge(S("grp_m"), 3 * gi + 3)
                for j in range(2):
                    last = V.tensor_tensor(ktr[:, 2 * j:2 * j + 2, :], bank2(2 + j),
                                           mask_k[:, :].unsqueeze(1).broadcast_to([P, 2, T]), ALU.mult)
                last.then_inc(S("ktr_ready"), 1)
                for l in range(1, 6):
                    ve.wait_ge(S("xt_ready"), 6 * gi + l)
                    ve.wait_ge(S("x_ready"), 6 * gi + l)
                    if l < 5:
                        ve.wait_ge(S("xp"), 4 * gi + l)
                        V.tensor_tensor(x_inv, x_inv, B(7).rearrange("p (q t) -> p q t", q=4), ALU.subtract)\
                            .then_inc(S("x_ready"), 1)
                    else:
                        ve.sem_inc(S("x_ready"), 1)
                    ve.wait_ge(S("xtp"), 5 * gi + l)
                    V.tensor_tensor(xt_inv, xt_inv, B(4).rearrange("p (q t) -> p q t", q=4), ALU.subtract)\
                        .then_inc(S("xt_ready"), 1)
                ve.wait_ge(S("w_done"), 2 * gi + 2)
                V.tensor_tensor(uu, w1, B(7)[:, 0:T].rearrange("p (q t) -> p q t", q=4), ALU.subtract)\
                    .then_inc(S("u_ready"), 1)
                if c == 0:
                    ve.wait_ge(S("send_done"), gi + 1)
                    ve.wait_ge(*at("fac_ready"))
                    V.tensor_tensor(s0[:, 2 * hh:2 * hh + 2, :], B(6)[:, 0:P].rearrange("p (q t) -> p q t", q=2),
                                    fac[:, 2 * hh:2 * hh + 2].unsqueeze(2).broadcast_to([P, 2, HD]), ALU.mult)\
                        .then_inc(S("s0_ready"), 1)
            yr = yT[:, 0:RT, :]
            gmean = view(tok_f, 1024, [RT, T])
            ve.wait_ge(*at("gn_meanc"))
            V.tensor_tensor(yr, yr, gmean, ALU.subtract).then_inc(*mark("gn_cent"))
            ve.wait_ge(*at("gn_rs"))
            ch.link(V.reciprocal(gmean, gmean))
            ve.wait_ge(*at("gn_cent"))
            ch.link(V.tensor_tensor(yr, yr, gmean, ALU.mult))
            for m in range(RT):
                ch.add(V.tensor_scalar(yT[:, m, :], yT[:, m, :], col("ln_g", m), col("ln_b", m), ALU.mult, ALU.add))
            ch.wait()
            ch.link(V.tensor_tensor(yr, yr, bonus, ALU.add))
            V.tensor_tensor(yr, yr, gT, ALU.mult).then_inc(*mark("y_ready"))
            ve.wait_ge(*at("y_ready"))
            ve.sem_inc(S("work_space_free"), 1)
            for b in range(4):
                ve.wait_ge(S("halves_used"), 2 * 19 + b + 1)
                for jj in range(2):
                    k = 2 * b + jj
                    last = V.scalar_tensor_tensor(out=xT[:, k, :], in0=bank2(4 + b)[:, jj, :],
                                                  scalar=mods[:, 16 + k:17 + k], in1=xT[:, k, :],
                                                  op0=ALU.mult, op1=ALU.add)
            last.then_inc(*mark("x2_ready"))
            ve.wait_ge(S("rs_ready"), 2)
            ch.link(V.reciprocal(rstd[:, :], rstd[:, :]))
            ve.wait_ge(*at("x2_ready"))
            V.tensor_tensor(hT[:, :, :], xT[:, :, :], rb, ALU.mult).then_inc(S("xn_ready"), 1)
            ve.wait_ge(*at("logits"))
            ch.link(V.tensor_copy(logit[:, :, :], B(1)[:, 0:TT * E_N].rearrange("p (i e) -> p i e", i=TT)))
            for i in range(TT):
                ch.add(V.max(top8[:, i, :], logit[:, i, :]))
            ch.wait()
            ch.add(V.tensor_scalar(small[:, 40:42], top8[:, :, 0], -1.0, None, ALU.mult))
            for i in range(TT):
                ch.add(V.tensor_scalar(wt[:, i, :], logit[:, i, :], top8[:, i, 3:4], None, ALU.is_gt))
                ch.add(V.tensor_scalar(selm[:, i, :], logit[:, i, :], top8[:, i, 3:4], None, ALU.is_equal))
            ch.wait()
            for i in range(TT):
                ch.add(V.tensor_reduce(small[:, 44 + i:45 + i], wt[:, i, :], AX.X, ALU.add))
                ch.add(V.tensor_tensor_scan(posm[:, i, :], ones[:, 0:E_N], selm[:, i, :], 0.0, ALU.mult, ALU.add))
            ch.wait()
            ch.link(V.tensor_scalar(small[:, 46:48], small[:, 44:46], -1.0, 4.0, ALU.mult, ALU.add))
            for i in range(TT):
                ch.add(V.tensor_scalar(posm[:, i, :], posm[:, i, :], small[:, 46 + i:47 + i], None, ALU.is_le))
            ch.wait()
            ch.link(V.tensor_tensor(selm[:, :, :], selm[:, :, :], posm[:, :, :], ALU.mult))
            V.tensor_tensor(selm[:, :, :], selm[:, :, :], wt[:, :, :], ALU.add).then_inc(*mark("sel_mask"))
            for b in (1, 3):
                ve.wait_ge(S("h2_turned"), b + 1)
                V.tensor_copy(tok[:, :, 2 * b * P:(2 * b + 2) * P], B(4 + b).rearrange("p (i x) -> p i x", i=2))\
                    .then_inc(S("h2tok_d"), 1)
            ve.wait_ge(*at("prob_e"))
            ve.wait_ge(*at("sel_mask"))
            ch.link(V.tensor_tensor(wt[:, :, :], prob[:, :, :], selm[:, :, :], ALU.mult))
            ch.link(V.tensor_reduce(small[:, 44:46], wt[:, :, :], AX.X, ALU.add))
            ch.link(V.reciprocal(small[:, 46:48], small[:, 44:46]))
            V.tensor_tensor(wt[:, :, :], wt[:, :, :], small[:, 46:48].unsqueeze(2).broadcast_to([P, TT, E_N]),
                            ALU.mult).then_inc(*mark("wt_ready"))
            ve.wait_ge(*at("ranks"))
            ch.link(V.scalar_tensor_tensor(out=posm[:, :, :], in0=B(2)[:, 0:TT * E_N].rearrange("p (i e) -> p i e", i=TT),
                                           scalar=1.0, in1=selm[:, :, :], op0=ALU.add, op1=ALU.mult))
            ch.add(V.tensor_scalar(posm[:, :, :], posm[:, :, :], -1.0, None, ALU.add))
            n_more = T // CAP - 1
            for r in range(n_more):
                ch.add(V.tensor_scalar(cnt[:, r, :], B(3)[0:1, 0:E_N], CAP * (r + 1) + 0.5, None, ALU.is_gt))
            ch.wait()
            for r in range(1, n_more):
                ch.link(V.tensor_tensor(cnt[:, 0, :], cnt[:, 0, :], cnt[:, r, :], ALU.add))
            ch.link(V.tensor_scalar(cnt[:, 0, :], cnt[:, 0, :], 1.0, None, ALU.add))
            ch.add(V.tensor_copy(npass[:, :], cnt[:, 0, :]))
            ch.link(V.tensor_tensor_scan(cnt[:, 1, :], ones[0:1, 0:E_N], cnt[:, 0, :], 0.0, ALU.mult, ALU.add))
            ch.add(V.tensor_copy(cum[:, :], cnt[:, 1, :]))
            ch.link(V.tensor_scalar(last_pass[:, :], cnt[:, 1, :], -1.0, None, ALU.add))
            ve.sem_inc(*mark("npass_ready"))
            ch.add(V.memset(ye, 0.0))
            ch.link(V.memset(selT, 0.0))
            ve.sem_inc(*mark("zeroed"))
            ve.wait_ge(*at("wt_turned"))
            V.tensor_copy(gt[0:E_N, 0:T], B(0)[0:E_N, 0:T]).then_inc(*mark("wtT_ready"))

            def select(e, p):
                for ti in range(TT):
                    last = V.tensor_scalar(sel[:, ti, :], iota[:, bass.ds(p * CAP, CAP)],
                                           posm[:, ti, bass.ds(e, 1)], None, ALU.is_equal)
                last.then_inc(S("e_sel"), 1)

            def expert_row(e):
                V.tensor_scalar(one_e, ones[0:E_N, 0:CAP], ident[0:E_N, bass.ds(e, 1)], None, ALU.mult)\
                    .then_inc(S("e_one"), 1)

            def select_weighted(e, p):
                for ti in range(TT):
                    last = V.tensor_scalar(selw[:, ti, :, :],
                                           iota[:, bass.ds(p * CAP, CAP)].unsqueeze(1).broadcast_to([P, 2, CAP]),
                                           posm[:, ti, bass.ds(e, 1)], wt[:, ti, bass.ds(e, 1)],
                                           ALU.is_equal, ALU.mult)
                last.then_inc(S("e_selw"), 1)

            ve.sem_inc(S("e_selT"), 1)
            select(0, 0)
            expert_row(0)
            select_weighted(0, 0)
            ch.link(V.tensor_tensor(ended, cnt[:, 1:2, :].broadcast_to([1, N_ITEM, E_N]),
                                    iota[0:1, 0:N_ITEM].unsqueeze(2).broadcast_to([1, N_ITEM, E_N]), ALU.is_le))
            ch.link(V.tensor_reduce(item_f[:, :], ended, AX.X, ALU.add))
            ch.add(V.tensor_scalar(item_e[:, :], item_f[:, :], E_N - 1.0, None, ALU.min))
            ch.link(V.tensor_tensor(ended, ended, cnt[:, 0:1, :].broadcast_to([1, N_ITEM, E_N]), ALU.mult))
            ch.link(V.tensor_reduce(item_f[:, :], ended, AX.X, ALU.add))
            ch.link(V.tensor_tensor(item_p[:, :], iota[0:1, 0:N_ITEM], item_f[:, :], ALU.subtract))
            total = ve.value_load(cum[0:1, E_N - 1:E_N], min_val=E_N, max_val=N_ITEM - 1)
            with ve.Fori(0, total) as g:
                e = ve.value_load(item_e[0:1, bass.ds(g + 1, 1)], min_val=0, max_val=E_N - 1)
                p = ve.value_load(item_p[0:1, bass.ds(g + 1, 1)], min_val=0, max_val=T // CAP - 1)
                ve.wait_ge(S("e_gather"), g + 1)
                select(e, p)
                ve.wait_ge(S("e_gu"), g * 2 + 1)
                V.tensor_scalar(gt, B(1), 7.0, None, ALU.min).then_inc(S("e_gate"), 1)
                ve.wait_ge(S("e_gu"), g * 2 + 2)
                V.tensor_scalar(ut, B(2), 7.0, -7.0, ALU.min, ALU.max).then_inc(S("e_up"), 1)
                ve.wait_ge(S("e_gate"), g + 1)
                ve.wait_ge(S("e_up"), g + 1)
                V.scalar_tensor_tensor(out=ut, in0=ut, scalar=1.0, in1=gt, op0=ALU.add, op1=ALU.mult)\
                    .then_inc(S("e_prod"), 1)
                ve.wait_ge(S("e_prod"), g + 1)
                ve.wait_ge(S("e_sig"), g + 1)
                V.tensor_tensor(act_tm, ut, sgm, ALU.mult).then_inc(S("e_act"), 1)
                expert_row(e)
                ve.wait_ge(S("e_selturn"), g + 1)
                V.tensor_copy(selT, B(1)[:, 0:T]).then_inc(S("e_selT"), 1)
                select_weighted(e, p)

            ve.wait_ge(S("moe_done"), 1)
            for k in range(KT):
                last = V.scalar_tensor_tensor(out=xT[:, k, :], in0=bank2(4 + k // 2)[:, k % 2, :],
                                              scalar=mods[:, 40 + k:41 + k], in1=xT[:, k, :],
                                              op0=ALU.mult, op1=ALU.add)
            last.then_inc(*mark("x3_ready"))
            for i in range(6):
                b = [(4, 5), (0, 1)][i % 2]
                ve.wait_ge(S("sb_ln"), i + 1)
                if i:
                    ve.wait_ge(S("sb_acc"), i)
                ch.link(V.tensor_scalar(sp, zs, 0.0, None, ALU.max))
                ch.link(V.tensor_tensor(sp, sp, ee, ALU.add))
                V.tensor_tensor(sp, sp, sb_mask[:, :].unsqueeze(1).broadcast_to([P, 2, 3 * P]), ALU.mult)\
                    .then_inc(S("sb_sp"), 1)
                ve.wait_ge(S("sb_acc"), i + 1)
                if i:
                    ve.wait_ge(S("sb_o"), i)
                for par_ in range(2):
                    ch.add(V.tensor_tensor(dd[:, par_, :], zs[:, par_, :], B(6 + par_)[:, 0:3 * P], ALU.subtract))
                ch.wait()
                V.scalar_tensor_tensor(out=dd, in0=dd, scalar=0.0,
                                       in1=sb_neg[:, :].unsqueeze(1).broadcast_to([P, 2, 3 * P]),
                                       op0=ALU.min, op1=ALU.add).then_inc(S("sb_d"), 1)
            for i in range(2):
                ve.wait_ge(S("mem_s"), i + 1)
                for par_ in range(2):
                    ch.add(V.tensor_reduce(small[:, 24 + 2 * par_:26 + 2 * par_], bank2(4 + par_), AX.X, ALU.max))
                ch.wait()
                V.tensor_scalar(small[:, 16:20], small[:, 24:28], -ATT_SCALE, None, ALU.mult).then_inc(S("mem_m"), 1)
                ve.wait_ge(S("mem_e"), i + 1)
                ch.link(V.reciprocal(small[:, 28:32], small[:, 20:24]))
                msv = ms.rearrange("p a b t -> p (a b) t")
                V.tensor_tensor(msv, msv, small[:, 28:32].unsqueeze(2).broadcast_to([P, 4, T]), ALU.mult)\
                    .then_inc(S("mem_p"), 1)

            def ln(r):
                for b in range(4):
                    if r == 0:
                        ve.wait_ge(S("halves_used"), 2 * (N_PRO + 6) + b + 1)
                    else:
                        ve.wait_ge(S("halves_used"), 2 * (N_PRO + N_POST))
                    last = V.scalar_tensor_tensor(out=xT[:, 2 * b:2 * b + 2, :], in0=xT[:, 2 * b:2 * b + 2, :],
                                                  scalar=ALPHA, in1=bank2(4 + b), op0=ALU.mult, op1=ALU.add)
                last.then_inc(S("ln_z"), 1)
                ve.wait_ge(S("ln_meanc"), r + 1)
                ve.wait_ge(S("ln_z"), r + 1)
                V.tensor_tensor(xT[:, :, :], xT[:, :, :], rb, ALU.subtract).then_inc(S("ln_cent"), 1)
                ve.wait_ge(S("ln_rs"), r + 1)
                ch.link(V.reciprocal(rstd[:, :], rstd[:, :]))
                ve.wait_ge(S("ln_cent"), r + 1)
                V.tensor_tensor(xT[:, :, :], xT[:, :, :], rb, ALU.mult).then_inc(S("ln_scaled"), 1)

            ln(0)
            for job in range(16):
                ve.wait_ge(S("up_relu"), job + 1)
                V.tensor_tensor(hid[:, 2 * job:2 * job + 2, :], fr[:, job % 2, :, :], fr[:, job % 2, :, :], ALU.mult)\
                    .then_inc(S("up_read"), 1)
            ln(1)
            for b in (1, 3):
                ve.wait_ge(S("out_turned"), b + 1)
                V.tensor_copy(tok[:, :, 2 * b * P:(2 * b + 2) * P], B(4 + b).rearrange("p (i x) -> p i x", i=2))\
                    .then_inc(S("out_ready_d"), 1)


N_PAR_DMA = 11 + 2 + 4 + 4

_UNUSED = ("w_in_hg_2", "lower_bounds_2", "hg_norm_g_2")


def kernel(**inputs):
    import concourse.bacc as bacc
    from concourse.bass_utils import run_bass_kernel_spmd

    nc = bacc.Bacc("TRN2", target_bir_lowering=False, num_devices=1)
    arrays, aps = {}, {}
    for name, value in inputs.items():
        if name in _UNUSED:
            continue
        v = np.ascontiguousarray(value)
        arrays["in_" + name] = v
        aps[name] = nc.dram_tensor("in_" + name, v.shape, F32, kind="ExternalInput").ap()
    out = nc.dram_tensor("out_0", (1, T, D), F32, kind="ExternalOutput").ap()
    build(nc, aps, out)
    r = run_bass_kernel_spmd(nc, [arrays], core_ids=[0])
    return r.results[0]["out_0"]
```
